# Optimizing a Trainium2 kernel written in Bass

```python
import math
import jax, jax.numpy as jnp
from jax import lax
import numpy as np

D_MODEL = 1024
BATCH = 1
SEQ = 1024
DEPTH = 1

N_MIXERS = 3
N_RET = (DEPTH + 2) // N_MIXERS
N_GDN = (DEPTH + 1) // N_MIXERS
N_SSD = DEPTH // N_MIXERS
D_FF = 4 * D_MODEL
NORM_EPS = 1e-6
CONV_K = 4

RET_HEADS = 4
RET_DK = D_MODEL // RET_HEADS
RET_DV = 2 * D_MODEL // RET_HEADS
RET_QK = RET_HEADS * RET_DK
RET_V = RET_HEADS * RET_DV
RET_IN = 2 * RET_QK + 2 * RET_V
RET_CHUNK = 128
RET_ROPE_BASE = 10000.0

GDN_QK_HEADS = 8
GDN_V_HEADS = 16
GDN_DK = 128
GDN_DV = 128
GDN_QK = GDN_QK_HEADS * GDN_DK
GDN_V = GDN_V_HEADS * GDN_DV
GDN_CONV_CH = 2 * GDN_QK + GDN_V
GDN_IN = GDN_CONV_CH + GDN_V + 2 * GDN_V_HEADS
GDN_CHUNK = 64

SSD_D_INNER = 2 * D_MODEL
SSD_HEAD_DIM = 64
SSD_HEADS = SSD_D_INNER // SSD_HEAD_DIM
SSD_GROUPS = 8
SSD_STATE = 128
SSD_CONV_CH = SSD_D_INNER + 2 * SSD_GROUPS * SSD_STATE
SSD_IN = SSD_D_INNER + SSD_CONV_CH + SSD_HEADS
SSD_CHUNK = 128

kernel_name = 'hybrid_ret_gdn_ssd_adaln_trunk'

def to_chunks(t, size):
    b, s = t.shape[:2]
    return jnp.moveaxis(t.reshape(b, s // size, size, *t.shape[2:]), 1, 0)

def from_chunks(t):
    n, b, size = t.shape[:3]
    return jnp.moveaxis(t, 0, 1).reshape(b, n * size, *t.shape[3:])

def rms_norm(x, g=None):
    xf = x.astype(jnp.float32)
    y = xf * lax.rsqrt(jnp.mean(xf * xf, axis=-1, keepdims=True) + NORM_EPS)
    if g is not None:
        y = y * g.astype(jnp.float32)
    return y.astype(x.dtype)

def l2_normalize(x):
    return x * lax.rsqrt(jnp.sum(x * x, axis=-1, keepdims=True) + 1e-6)

def causal_dwconv(x, w):
    k = w.shape[0]
    return lax.conv_general_dilated(x, w[:, None, :].astype(x.dtype), window_strides=(1,), padding=[(k - 1, 0)], dimension_numbers=('NWC', 'WIO', 'NWC'), feature_group_count=x.shape[-1])

def rotate_pairs(x, cos, sin):
    x1 = x[..., 0::2]
    x2 = x[..., 1::2]
    return jnp.stack([x1 * cos - x2 * sin, x1 * sin + x2 * cos], axis=-1).reshape(x.shape)

def retention_scan(q, k, v):
    b, s, nh, dk = q.shape
    dv = v.shape[-1]
    c = RET_CHUNK
    lg = jnp.log1p(-jnp.exp2(-5.0 - jnp.arange(nh, dtype=jnp.float32)))
    pos = jnp.arange(c, dtype=jnp.float32)
    rel = pos[:, None] - pos[None, :]
    causal = rel >= 0
    dmask = jnp.where(causal, jnp.exp(jnp.where(causal, rel, 0.0) * lg[:, None, None]), 0.0)
    xi = jnp.exp((pos[:, None] + 1.0) * lg[None, :])
    zeta = jnp.exp((c - 1.0 - pos)[:, None] * lg[None, :])
    decay_c = jnp.exp(c * lg)

    def step(r, inp):
        qc, kc, vc = inp
        sc = jnp.einsum('bthd,bshd->bhts', qc, kc) * dmask
        o = jnp.einsum('bhts,bshv->bthv', sc, vc) + jnp.einsum('bthd,bhdv->bthv', qc, r) * xi[None, :, :, None]
        r = r * decay_c[None, :, None, None] + jnp.einsum('bshd,bshv->bhdv', kc * zeta[None, :, :, None], vc)
        return r, o

    r0 = jnp.zeros((b, nh, dk, dv), jnp.float32)
    _, o = lax.scan(step, r0, (to_chunks(q, c), to_chunks(k, c), to_chunks(v, c)))
    return from_chunks(o)

def retention(h, w_in, w_out):
    b, s, _ = h.shape
    q, k, v, g = jnp.split(h @ w_in, [RET_QK, 2 * RET_QK, 2 * RET_QK + RET_V], axis=-1)
    q = q.reshape(b, s, RET_HEADS, RET_DK).astype(jnp.float32)
    k = k.reshape(b, s, RET_HEADS, RET_DK).astype(jnp.float32)
    v = v.reshape(b, s, RET_HEADS, RET_DV).astype(jnp.float32)
    inv_freq = RET_ROPE_BASE ** (-jnp.linspace(0.0, 1.0, RET_DK // 2, dtype=jnp.float32))
    ang = jnp.arange(s, dtype=jnp.float32)[:, None] * inv_freq[None, :]
    cos = jnp.cos(ang)[None, :, None, :]
    sin = jnp.sin(ang)[None, :, None, :]
    q = rotate_pairs(q, cos, sin)
    k = rotate_pairs(k, cos, sin) * (RET_DK ** -0.5)
    o = retention_scan(q, k, v)
    o = rms_norm(o).reshape(b, s, RET_V).astype(h.dtype)
    return (jax.nn.silu(g) * o) @ w_out

def gated_delta_scan(q, k, v, beta, g):
    b, s, nh, dk = q.shape
    dv = v.shape[-1]
    c = GDN_CHUNK
    incl = jnp.tril(jnp.ones((c, c), bool))
    strict = jnp.tril(jnp.ones((c, c), bool), -1)
    eye = jnp.eye(c, dtype=jnp.float32)

    def step(st, inp):
        qc, kc, vc, bc, gc = inp
        gcum = jnp.cumsum(gc, axis=1)
        gh = jnp.swapaxes(gcum, 1, 2)
        rel = gh[..., :, None] - gh[..., None, :]
        decay = jnp.where(incl, jnp.exp(jnp.where(incl, rel, 0.0)), 0.0)
        kb = kc * bc[..., None]
        a_mat = jnp.einsum('bthd,bshd->bhts', kb, kc) * decay
        lmat = eye + jnp.where(strict, a_mat, 0.0)
        rhs = jnp.concatenate([vc * bc[..., None], kb * jnp.exp(gcum)[..., None]], axis=-1)
        sol = lax.linalg.triangular_solve(lmat, jnp.swapaxes(rhs, 1, 2), left_side=True, lower=True, unit_diagonal=True)
        u, w = sol[..., :dv], sol[..., dv:]
        v_new = u - jnp.einsum('bhtd,bhdv->bhtv', w, st)
        qk = jnp.einsum('bthd,bshd->bhts', qc, kc) * decay
        q_dec = jnp.swapaxes(qc * jnp.exp(gcum)[..., None], 1, 2)
        o = jnp.einsum('bhtd,bhdv->bhtv', q_dec, st) + jnp.einsum('bhts,bhsv->bhtv', qk, v_new)
        g_last = gh[..., -1]
        k_dec = kc * jnp.exp(g_last[:, None, :] - gcum)[..., None]
        st = st * jnp.exp(g_last)[..., None, None] + jnp.einsum('bshd,bhsv->bhdv', k_dec, v_new)
        return st, jnp.swapaxes(o, 1, 2)

    st0 = jnp.zeros((b, nh, dk, dv), jnp.float32)
    _, o = lax.scan(step, st0, (to_chunks(q, c), to_chunks(k, c), to_chunks(v, c), to_chunks(beta, c), to_chunks(g, c)))
    return from_chunks(o)

def gated_deltanet(h, w_in, conv_w, a_log, dt_bias, norm_g, w_out):
    b, s, _ = h.shape
    qkv, z, beta_in, a_in = jnp.split(h @ w_in, [GDN_CONV_CH, GDN_CONV_CH + GDN_V, GDN_CONV_CH + GDN_V + GDN_V_HEADS], axis=-1)
    qkv = jax.nn.silu(causal_dwconv(qkv, conv_w))
    q, k, v = jnp.split(qkv, [GDN_QK, 2 * GDN_QK], axis=-1)
    rep = GDN_V_HEADS // GDN_QK_HEADS
    q = jnp.repeat(q.reshape(b, s, GDN_QK_HEADS, GDN_DK), rep, axis=2).astype(jnp.float32)
    k = jnp.repeat(k.reshape(b, s, GDN_QK_HEADS, GDN_DK), rep, axis=2).astype(jnp.float32)
    v = v.reshape(b, s, GDN_V_HEADS, GDN_DV).astype(jnp.float32)
    q = l2_normalize(q) * (GDN_DK ** -0.5)
    k = l2_normalize(k)
    beta = jax.nn.sigmoid(beta_in.astype(jnp.float32))
    g = -jnp.exp(a_log.astype(jnp.float32)) * jax.nn.softplus(a_in.astype(jnp.float32) + dt_bias.astype(jnp.float32))
    o = gated_delta_scan(q, k, v, beta, g)
    o = rms_norm(o, norm_g) * jax.nn.silu(z.reshape(b, s, GDN_V_HEADS, GDN_DV).astype(jnp.float32))
    return o.reshape(b, s, GDN_V).astype(h.dtype) @ w_out

def ssd_scan(x, dt, a, bm, cm):
    b, s, nh, p = x.shape
    ng, n = bm.shape[2:]
    j = nh // ng
    c = SSD_CHUNK
    incl = jnp.tril(jnp.ones((c, c), bool))

    def step(st, inp):
        xc, dtc, bc, cc = inp
        acum = jnp.cumsum(dtc * a, axis=1)
        ah = jnp.moveaxis(acum, 1, 2).reshape(b, ng, j, c)
        rel = ah[..., :, None] - ah[..., None, :]
        seg = jnp.where(incl, jnp.exp(jnp.where(incl, rel, 0.0)), 0.0)
        cb = jnp.einsum('btgn,bsgn->bgts', cc, bc)
        xdt = (xc * dtc[..., None]).reshape(b, c, ng, j, p)
        y_diag = jnp.einsum('bgjts,bsgjp->btgjp', cb[:, :, None] * seg, xdt)
        y_off = jnp.einsum('btgn,bgjpn->btgjp', cc, st) * jnp.exp(acum).reshape(b, c, ng, j)[..., None]
        a_last = ah[..., -1]
        w_dec = jnp.exp(a_last[..., None] - ah)
        st = st * jnp.exp(a_last)[..., None, None] + jnp.einsum('bsgn,bgjs,bsgjp->bgjpn', bc, w_dec, xdt)
        return st, (y_diag + y_off).reshape(b, c, nh, p)

    st0 = jnp.zeros((b, ng, j, p, n), jnp.float32)
    _, y = lax.scan(step, st0, (to_chunks(x, c), to_chunks(dt, c), to_chunks(bm, c), to_chunks(cm, c)))
    return from_chunks(y)

def mamba2_ssd(h, w_in, conv_w, conv_b, a_log, dt_bias, d_skip, norm_g, w_out):
    b, s, _ = h.shape
    z, xbc, dt = jnp.split(h @ w_in, [SSD_D_INNER, SSD_D_INNER + SSD_CONV_CH], axis=-1)
    xbc = jax.nn.silu(causal_dwconv(xbc, conv_w) + conv_b)
    xs, bm, cm = jnp.split(xbc, [SSD_D_INNER, SSD_D_INNER + SSD_GROUPS * SSD_STATE], axis=-1)
    xs = xs.reshape(b, s, SSD_HEADS, SSD_HEAD_DIM).astype(jnp.float32)
    bm = bm.reshape(b, s, SSD_GROUPS, SSD_STATE).astype(jnp.float32)
    cm = cm.reshape(b, s, SSD_GROUPS, SSD_STATE).astype(jnp.float32)
    dt = jax.nn.softplus(dt.astype(jnp.float32) + dt_bias.astype(jnp.float32))
    a = -jnp.exp(a_log.astype(jnp.float32))
    y = ssd_scan(xs, dt, a, bm, cm) + d_skip.astype(jnp.float32)[:, None] * xs
    y = y.reshape(b, s, SSD_D_INNER) * jax.nn.silu(z.astype(jnp.float32))
    y = rms_norm(y.reshape(b, s, SSD_GROUPS, SSD_D_INNER // SSD_GROUPS)).reshape(b, s, SSD_D_INNER) * norm_g.astype(jnp.float32)
    return y.astype(h.dtype) @ w_out

def squared_relu_mlp(h, w1, w2):
    return jnp.square(jax.nn.relu(h @ w1)) @ w2

def _dt_bias(key, shape):
    dt = jnp.exp(jax.random.uniform(key, shape, jnp.float32, math.log(1e-3), math.log(1e-1)))
    return dt + jnp.log(-jnp.expm1(-dt))

def setup_inputs(seed: int = 0) -> dict:
    key = jax.random.key(seed)
    ks = jax.random.split(key, 26)

    def nrm(i, shape, scale):
        return jax.random.normal(ks[i], shape, jnp.float32) * scale

    return {
        'x': nrm(0, (BATCH, SEQ, D_MODEL), 1.0),
        'c': nrm(1, (BATCH, D_MODEL), 1.0),
        'ada_w': nrm(2, (DEPTH, D_MODEL, 6 * D_MODEL), 0.1 * D_MODEL ** -0.5),
        'ada_b': nrm(3, (DEPTH, 6 * D_MODEL), 0.01),
        'norm_mix_g': 1.0 + nrm(4, (DEPTH, D_MODEL), 0.02),
        'norm_mlp_g': 1.0 + nrm(5, (DEPTH, D_MODEL), 0.02),
        'mlp_w1': nrm(6, (DEPTH, D_MODEL, D_FF), D_MODEL ** -0.5),
        'mlp_w2': nrm(7, (DEPTH, D_FF, D_MODEL), D_FF ** -0.5),
        'final_norm_g': 1.0 + nrm(8, (D_MODEL,), 0.02),
        'ret_w_in': nrm(9, (N_RET, D_MODEL, RET_IN), D_MODEL ** -0.5),
        'ret_w_out': nrm(10, (N_RET, RET_V, D_MODEL), RET_V ** -0.5),
        'gdn_w_in': nrm(11, (N_GDN, D_MODEL, GDN_IN), D_MODEL ** -0.5),
        'gdn_conv_w': nrm(12, (N_GDN, CONV_K, GDN_CONV_CH), CONV_K ** -0.5),
        'gdn_A_log': jnp.log(jax.random.uniform(ks[13], (N_GDN, GDN_V_HEADS), jnp.float32, 1.0, 16.0)),
        'gdn_dt_bias': _dt_bias(ks[14], (N_GDN, GDN_V_HEADS)),
        'gdn_norm_g': 1.0 + nrm(15, (N_GDN, GDN_DV), 0.02),
        'gdn_w_out': nrm(16, (N_GDN, GDN_V, D_MODEL), GDN_V ** -0.5),
        'ssd_w_in': nrm(17, (N_SSD, D_MODEL, SSD_IN), D_MODEL ** -0.5),
        'ssd_conv_w': nrm(18, (N_SSD, CONV_K, SSD_CONV_CH), CONV_K ** -0.5),
        'ssd_conv_b': nrm(19, (N_SSD, SSD_CONV_CH), 0.01),
        'ssd_A_log': jnp.log(jax.random.uniform(ks[20], (N_SSD, SSD_HEADS), jnp.float32, 1.0, 16.0)),
        'ssd_dt_bias': _dt_bias(ks[21], (N_SSD, SSD_HEADS)),
        'ssd_D': 1.0 + nrm(22, (N_SSD, SSD_HEADS), 0.1),
        'ssd_norm_g': 1.0 + nrm(23, (N_SSD, SSD_D_INNER), 0.02),
        'ssd_w_out': nrm(24, (N_SSD, SSD_D_INNER, D_MODEL), SSD_D_INNER ** -0.5),
    }

def reference(x, c, ada_w, ada_b, norm_mix_g, norm_mlp_g, mlp_w1, mlp_w2, final_norm_g, ret_w_in, ret_w_out, gdn_w_in, gdn_conv_w, gdn_A_log, gdn_dt_bias, gdn_norm_g, gdn_w_out, ssd_w_in, ssd_conv_w, ssd_conv_b, ssd_A_log, ssd_dt_bias, ssd_D, ssd_norm_g, ssd_w_out):
    cond = jax.nn.silu(c)
    for l in range(DEPTH):
        mod = cond @ ada_w[l] + ada_b[l]
        sh1, sc1, gt1, sh2, sc2, gt2 = [m[:, None, :] for m in jnp.split(mod, 6, axis=-1)]
        h = rms_norm(x, norm_mix_g[l]) * (1.0 + sc1) + sh1
        kind = l % N_MIXERS
        j = l // N_MIXERS
        if kind == 0:
            y = retention(h, ret_w_in[j], ret_w_out[j])
        elif kind == 1:
            y = gated_deltanet(h, gdn_w_in[j], gdn_conv_w[j], gdn_A_log[j], gdn_dt_bias[j], gdn_norm_g[j], gdn_w_out[j])
        else:
            y = mamba2_ssd(h, ssd_w_in[j], ssd_conv_w[j], ssd_conv_b[j], ssd_A_log[j], ssd_dt_bias[j], ssd_D[j], ssd_norm_g[j], ssd_w_out[j])
        x = x + (1.0 + gt1) * y
        h = rms_norm(x, norm_mlp_g[l]) * (1.0 + sc2) + sh2
        x = x + (1.0 + gt2) * squared_relu_mlp(h, mlp_w1[l], mlp_w2[l])
    return rms_norm(x, final_norm_g)


_drawn_inputs = setup_inputs


def setup_inputs(seed=0):
    import zlib

    import numpy as np

    out = dict(_drawn_inputs(seed))
    spreads = {}
    factors = {'norm_mlp_g': 3.246, 'final_norm_g': 2.986}
    for name, (base, spread) in spreads.items():
        noise = np.random.default_rng([zlib.crc32(name.encode()), seed]).standard_normal(out[name].shape)
        drawn = base * np.exp(spread * noise) if base else spread * noise
        out[name] = __import__('jax').numpy.asarray(drawn.astype(out[name].dtype))
    for name, factor in factors.items():
        out[name] = (out[name] * factor).astype(out[name].dtype)
    return out
```

```python
import math
from contextlib import ExitStack

import numpy as np
import concourse.bass as bass
from concourse import mybir

F32 = mybir.dt.float32
F32R = mybir.dt.float32r
ALU = mybir.AluOpType
ACT = mybir.ActivationFunctionType

P = 128
D = 1024
T = 1024
KT = D // P
HALF = 512
HEADS = 4
DK = D // HEADS
DV = 2 * D // HEADS
FF = 4 * D
CHUNK = 256
NCHUNK = T // CHUNK
TT = T // P
UNIT = 1024
STAGE_SLOTS = 4
SPLIT_SLOTS = 6
FLOW_SLOTS = 4
BLOCKS = FF // HALF
EPS = 1e-6

C_COND, C_ADAB, C_GMIX, C_GMLP, C_GFIN, N_VEC = 0, 8, 56, 64, 72, 80
H_MASK, H_EPS, H_ZETA, H_DECAY, N_HEAD = 0, 384, 386, 388, 390
M_SH1, M_SC1, M_GT1, M_SH2, M_SC2, M_GT2 = range(0, 48, 8)

ADA_FIRST = 2 * KT
HEAD_UNITS = 12
HEAD_STREAM = HEAD_UNITS + KT
STREAM = [("w", j) for j in range(2, 10)] + [("a", k) for k in range(KT)] + [("w", j) for j in range(10, 14)]
W_OUT0 = HEADS * HEAD_UNITS
W_MLP0 = W_OUT0 + 4 * HEADS


def constants():
    inv = np.float32(10000.0) ** (-np.linspace(0.0, 1.0, DK // 2, dtype=np.float32))
    ang = (np.arange(T, dtype=np.float32)[:, None] * inv[None, :].astype(np.float32)).astype(np.float32)
    rope = np.stack([np.cos(ang).T, np.sin(ang).T], axis=1).astype(np.float32)
    lg = np.log1p(-np.exp2(-5.0 - np.arange(HEADS)))
    s = np.arange(P)[:, None]
    t = np.arange(P)[None, :]
    tri = (s <= t).astype(np.float64)
    k_scale = DK ** -0.5
    heads = np.zeros((HEADS, P, N_HEAD))
    for h in range(HEADS):
        down = np.exp(-(s + 1.0) * lg[h]) * k_scale
        heads[h, :, 0:128] = tri * down
        heads[h, :, 128:256] = down
        heads[h, :, 256:384] = tri * np.exp(-(s + 129.0) * lg[h]) * k_scale
        for a in range(2):
            xi = np.exp((s[:, 0] + 128 * a + 1.0) * lg[h])
            heads[h, :, H_EPS + a] = DV * EPS / (xi * xi)
            heads[h, :, H_ZETA + a] = np.exp((CHUNK - 1.0 - 128 * a - s[:, 0]) * lg[h]) * k_scale
        heads[h, :, H_DECAY] = np.exp(CHUNK * lg[h])
    return rope, heads.astype(np.float32), np.eye(P, dtype=np.float32)


def build(nc, xT, vec, ada, weights, rope, heads, eye, outT):
    ctx = ExitStack()
    with ctx:
        def sem(name):
            return ctx.enter_context(nc.semaphore(name))

        def sb(name, shape, dt=F32, into=ctx):
            return into.enter_context(nc.sbuf_tensor(name, shape, dt))

        ht = sb("ht", [P, 2, KT, T], F32R)
        stage = sb("stage", [P, STAGE_SLOTS, UNIT])
        wsplit = sb("wsplit", [P, SPLIT_SLOTS, 2, UNIT], F32R)
        vecs = sb("vecs", [P, N_VEC])
        mods = sb("mods", [P, 48])
        gains = sb("gains", [P, 4, KT])
        cond = sb("cond", [P, KT])
        ident = sb("ident", [P, P])
        ones = sb("ones", [P, P])
        power = sb("power", [P, KT])
        zcol = sb("zcol", [P, KT])
        rcol = sb("rcol", [P, KT])

        first = ExitStack()
        qkv = sb("qkv", [P, 8, T], into=first)
        og = sb("og", [P, TT, DV], into=first)
        trig = sb("trig", [P, 2, T], into=first)
        sc = sb("sc", [P, 2, 384], into=first)
        kn = sb("kn", [P, 2, 2, DK], into=first)
        state = sb("state", [P, 2, 2, DV], into=first)
        hc = sb("hc", [P, N_HEAD], into=first)
        turned = sb("turned", [P, 2, DV], into=first)
        rs = sb("rs", [P, 3, 2], into=first)
        first.close()
        v = qkv[:, 4:8, :].rearrange("p a (b n) -> p (a b) n", n=DV)
        ogf = og[:, :, :].rearrange("p a n -> p (a n)")
        ada_sum = [ogf[:, i * UNIT:(i + 1) * UNIT] for i in range(2)]
        squares1 = [ogf[:, (2 + i) * UNIT:(3 + i) * UNIT] for i in range(2)]
        rope_tmp = [ogf[:, 2048 + i * HALF:2048 + (i + 1) * HALF] for i in range(4)]
        statef = state[:, :, :, :].rearrange("p a b n -> p (a b n)")
        diag1 = statef[:, 0:UNIT]
        tmp1 = [statef[:, UNIT + i * HALF:UNIT + (i + 1) * HALF] for i in range(2)]

        second = ExitStack()
        x1 = sb("x1", [P, KT, T], into=second)
        ou = sb("ou", [P, 2, 4, T], F32R, into=second)
        ostage = sb("ostage", [P, 2, 2, DV], into=second)
        spare = sb("spare", [P, UNIT], into=second)
        second.close()
        ostf = ostage[:, :, :, :].rearrange("p a b n -> p (a b n)")
        squares2 = [ostf[:, i * UNIT:(i + 1) * UNIT] for i in range(2)]
        diag2 = spare[:, :]
        tmp2 = [ostf[:, i * HALF:(i + 1) * HALF] for i in range(4)]
        relu = [spare[:, i * HALF:(i + 1) * HALF] for i in range(2)]

        pp = [ctx.enter_context(nc.psum_tensor(f"pp{i}", [P, HALF], F32)) for i in range(4)]
        pa = [ctx.enter_context(nc.psum_tensor(f"pa{i}", [P, HALF], F32)) for i in range(4)]

        gated_dram = nc.dram_tensor("gated_T", (HEADS, TT, P, DV), F32, kind="Internal").ap()

        consts_in, trig_in = sem("consts_in"), sem("trig_in")
        x_in = [sem(f"x_in{k}") for k in range(KT)]
        staged = [sem(f"staged{i}") for i in range(STAGE_SLOTS)]
        taken = sem("taken")
        hi_made = sem("hi_made")
        setup_done = sem("setup_done")
        cond_done = sem("cond_done")
        ada_done = sem("ada_done")
        mods_done = sem("mods_done")
        gains_done = sem("gains_done")
        squared = sem("squared")
        sq_read = sem("sq_read")
        z_done, pow_done, diag_done, bc_done = sem("z_done"), sem("pow_done"), sem("diag_done"), sem("bc_done")
        scaled, ht_hi, ht_done = sem("scaled"), sem("ht_hi"), sem("ht_done")
        qk_done, qk_read, roped = sem("qk_done"), sem("qk_read"), sem("roped")
        v_done, v_read, v_unit_free = sem("v_done"), sem("v_read"), sem("v_unit_free")
        sc_done, sc_read = sem("sc_done"), sem("sc_read")
        kt_done, kt_read = sem("kt_done"), sem("kt_read")
        kv_done, state_done = sem("kv_done"), sem("state_done")
        o_done, o_squared, row_scale, o_read = sem("o_done"), sem("o_squared"), sem("row_scale"), sem("o_read")
        scale_step = sem("scale_step")
        g_done, silu_done, gated, g_unit_free = sem("g_done"), sem("silu_done"), sem("gated"), sem("g_unit_free")
        t_done, t_read = sem("t_done"), sem("t_read")
        hc_in = sem("hc_in")
        stored = [sem("stored0"), sem("stored1")]
        o_in = [sem("o_in0"), sem("o_in1")]
        o_hi, o_taken = sem("o_hi"), sem("o_taken")
        x1_in = sem("x1_in")
        wo_done, wo_read = sem("wo_done"), sem("wo_read")
        u_done, relu_done, u_sq, u_hi, u_read = sem("u_done"), sem("relu_done"), sem("u_sq"), sem("u_hi"), sem("u_read")
        y_done, y_read = sem("y_done"), sem("y_read")
        out_ready = sem("out_ready")
        out_stored = [sem(f"out_stored{i}") for i in range(4)]

        RING = 8

        block = ctx.enter_context(nc.Block())

        def head_pos(h, idx):
            return h * HEAD_STREAM + ADA_FIRST + 2 + idx

        def unit_pos(h, j):
            return h * HEAD_STREAM + ADA_FIRST + j + (KT if j in (10, 11, 12, 13) else 0)

        def later_pos(i):
            return i + ADA_FIRST + HEADS * HEAD_STREAM

        @block.sync
        def _(sp):
            def load(source, slot, p):
                sp.wait_ge(taken, p - STAGE_SLOTS + 1)
                sp.dma_start(stage[:, slot, :], source).then_inc(staged[slot], 16)

            sp.dma_start(vecs[:, :], vec).then_inc(consts_in, 16)
            sp.dma_start(ident[:, :], eye).then_inc(consts_in, 16)
            for p in range(ADA_FIRST):
                if p < STAGE_SLOTS:
                    sp.dma_start(stage[:, p, :], ada[p // KT, p % KT]).then_inc(staged[p], 16)
                else:
                    load(ada[p // KT, p % KT], p % STAGE_SLOTS, p)
                if p % 2 == 1:
                    sp.dma_start(qkv[:, p // 2, :], xT[p // 2]).then_inc(x_in[p // 2], 16)
            for j in range(2):
                load(weights[j], j, ADA_FIRST + j)
            sp.dma_start(trig[:, :, :], rope).then_inc(trig_in, 16)
            with sp.Fori(0, HEADS) as h:
                for idx, (kind, j) in enumerate(STREAM):
                    if idx == KT:
                        sp.wait_ge(row_scale, h * TT + 1)
                        sp.dma_start(hc[:, :], heads[h]).then_inc(hc_in, 16)
                    slot = (2 + idx) % STAGE_SLOTS
                    source = weights[h * HEAD_UNITS + j] if kind == "w" else ada[h + 2, j]
                    load(source, slot, head_pos(h, idx))
            for i in range(2, 16):
                if i == 2:
                    sp.wait_ge(t_done, TT * HEADS)
                    for k in range(KT):
                        sp.dma_start(x1[:, k, :], xT[k]).then_inc(x1_in, 16)
                load(weights[W_OUT0 + i], i % STAGE_SLOTS, later_pos(i))
            for j in range(8):
                load(weights[W_MLP0 + j], j % STAGE_SLOTS, later_pos(16 + j))
            with sp.Fori(1, BLOCKS) as b:
                for j in range(8):
                    load(weights[b * 8 + (W_MLP0 + j)], j % STAGE_SLOTS, b * 8 + later_pos(16 + j))
            for n in range(16):
                half, k = divmod(n, KT)
                sp.wait_ge(out_ready, n + 1)
                sp.dma_start(outT[k][:, half * HALF:(half + 1) * HALF], tmp2[n % 4]).then_inc(out_stored[n % 4], 16)
            for i in range(4):
                sp.wait_ge(out_stored[i], 16 * 4)

        @block.gpsimd
        def _(pool):
            pool.memset(power[:, :], -0.5).then_inc(setup_done, 1)
            pool.memset(ones[:, :], 1.0).then_inc(setup_done, 1)
            pool.wait_ge(setup_done, 2)

            def norm_power(n):
                pool.wait_ge(z_done, n)
                pool.tensor_tensor(rcol[:, :], zcol[:, :], power[:, :], ALU.pow).then_inc(pow_done, 1)

            norm_power(1)
            with pool.Fori(0, HEADS) as h:
                for i in range(TT):
                    a = i % 2
                    pool.wait_ge(o_squared, h * TT + (RING + i + 1))
                    if i == 0:
                        pool.wait_ge(hc_in, h * 16 + 16)
                    pool.tensor_tensor(rs[:, 1, a:a + 1], rs[:, 0, a:a + 1], hc[:, H_EPS + a:H_EPS + a + 1], ALU.add)\
                        .then_inc(scale_step, 1)
                    pool.wait_ge(scale_step, h * TT + (i + 1))
                    pool.tensor_tensor(rs[:, 2, a:a + 1], rs[:, 1, a:a + 1], power[:, 0:1], ALU.pow).then_inc(row_scale, 1)
            for a in range(2):
                pool.wait_ge(stored[a], 16 * (1 + 4 * HEADS))
            pool.wait_ge(t_done, TT * HEADS)
            for h in range(HEADS):
                for c in range(4):
                    n = 4 * h + c
                    if n >= 2:
                        pool.wait_ge(o_taken, n - 1)
                    pool.dma_start(ostage[:, n % 2, :, :], gated_dram[h, 2 * c:2 * c + 2].rearrange("a p n -> p a n"))\
                        .then_inc(o_in[n % 2], 16)
            norm_power(2)
            norm_power(3)

        @block.scalar
        def _(act):
            def split_hi(slot, split_slot, arrived):
                act.wait_ge(staged[slot], arrived)
                act.activation(wsplit[:, split_slot, 0, :], stage[:, slot, :], ACT.Copy).then_inc(hi_made, 1)

            def arrived(pos0):
                return 16 * (pos0 // STAGE_SLOTS + 1)

            def head_hi(h, j):
                if j in (2, 3, 4):
                    act.wait_ge(g_unit_free, h * 3 + (j - 1))
                elif j == 5:
                    act.wait_ge(g_done, h * TT + RING)
                elif j in (6, 7, 8, 9):
                    act.wait_ge(qk_done, h * TT + 2 * (j - 5))
                elif j in (10, 11, 12):
                    act.wait_ge(v_unit_free, h * 3 + (j - 9))
                else:
                    act.wait_ge(v_done, h * TT + TT)
                pos = unit_pos(0, j)
                split_hi(pos % STAGE_SLOTS, j % SPLIT_SLOTS, h * (16 * HEAD_STREAM // STAGE_SLOTS) + arrived(pos))

            def squares(n, source, ready, out):
                for k in range(KT):
                    act.wait_ge(*ready(k))
                    if KT * n + k >= 2:
                        act.wait_ge(sq_read, KT * n + k - 1)
                    act.activation(out[k % 2], source[:, k, :], ACT.Square).then_inc(squared, 1)

            def ht_write(n, tmp, shift):
                for i in range(16):
                    half, k = divmod(i, KT)
                    act.wait_ge(scaled, 16 * n + i + 1)
                    act.activation(ht[:, 0, k, half * HALF:(half + 1) * HALF], tmp[i % 2], ACT.Identity,
                                   bias=mods[:, shift + k:shift + k + 1]).then_inc(ht_hi, 1)

            act.wait_ge(consts_in, 32)
            act.activation(cond[:, :], vecs[:, C_COND:C_COND + KT], ACT.Silu).then_inc(cond_done, 1)
            squares(0, qkv, lambda k: (x_in[k], 16), squares1)
            for j in range(2):
                split_hi(j, j, arrived(ADA_FIRST + j))
            act.wait_ge(mods_done, 2)
            ht_write(0, tmp1, M_SH1)

            with act.Fori(0, HEADS) as h:
                for j in range(2, 10):
                    head_hi(h, j)
                for i in range(TT):
                    act.wait_ge(v_done, h * TT + (i + 1))
                    act.activation(v[:, i, :], pp[i % 4][:, :], ACT.Copy).then_inc(v_read, 1)

                def keys(c):
                    act.wait_ge(kt_done, h * 3 + (c + 1))
                    for a in range(2):
                        last = act.activation(kn[:, c % 2, a, :], pp[2 + c % 2][:, a * DK:(a + 1) * DK], ACT.Copy,
                                              scale=hc[:, H_ZETA + a:H_ZETA + a + 1])
                    last.then_inc(kt_read, 1)

                def square(i):
                    act.wait_ge(o_done, h * TT + (i + 1))
                    act.activation(og[:, i, :], pa[2 + i % 2][:, :], ACT.Square, accum_out=rs[:, 0, i % 2:i % 2 + 1])\
                        .then_inc(o_squared, 1)

                act.wait_ge(hc_in, h * 16 + 16)
                keys(0)
                keys(1)
                head_hi(h, 10)
                square(0)
                square(1)
                keys(2)
                head_hi(h, 11)
                square(2)
                square(3)
                head_hi(h, 12)
                square(4)
                square(5)
                head_hi(h, 13)
                square(6)
                square(7)

                def silu(i):
                    act.wait_ge(g_done, h * TT + (RING + i + 1))
                    act.activation(pp[i % 4][:, :], pp[i % 4][:, :], ACT.Silu).then_inc(silu_done, 1)

                def turned_out(i):
                    act.wait_ge(t_done, h * TT + (i + 1))
                    act.wait_ge(stored[i % 2], h * 64 + 16 * (i // 2 + 1))
                    act.activation(turned[:, i % 2, :], pa[i % 2][:, :], ACT.Copy).then_inc(t_read, 1)

                def store(i):
                    act.wait_ge(t_read, h * TT + (RING + i + 1))
                    act.dma_start(gated_dram[h, i], turned[:, i % 2, :]).then_inc(stored[i % 2], 16)

                silu(0)
                for i in range(1, TT):
                    silu(i)
                    turned_out(i - 1)
                    store(i - 1)
                turned_out(TT - 1)
                store(TT - 1)

            def later_hi(i):
                if i in (2, 3):
                    act.wait_ge(g_unit_free, 3 * HEADS + i - 1)
                else:
                    act.wait_ge(wo_done, 4 * (i - 3))
                pos = later_pos(i)
                split_hi(pos % STAGE_SLOTS, i % FLOW_SLOTS, arrived(pos))

            def o_split_hi(n):
                h, c = divmod(n, 4)
                act.wait_ge(o_in[n % 2], 16 * (n // 2 + 1))
                if c == 0 and h >= 2:
                    act.wait_ge(wo_done, 16 * (h - 1))
                dst = (ht[:, 0, 4:8, :] if h % 2 == 0 else ou[:, 0, :, :])[:, :, c * 256:(c + 1) * 256]
                act.activation(dst.rearrange("p d (a t) -> p d a t", a=2),
                               ostage[:, n % 2, :, :].rearrange("p a (d t) -> p d a t", d=4), ACT.Copy).then_inc(o_hi, 1)

            for n in range(4):
                o_split_hi(n)
            later_hi(2)
            later_hi(3)
            for n in range(4, 8):
                o_split_hi(n)
            for h in range(HEADS):
                for j in range(4):
                    later_hi(4 * h + 4 + j)
                    if j == 3 and h < 2:
                        for n in range(4 * h + 8, 4 * h + 12):
                            o_split_hi(n)

            act.wait_ge(wo_read, 64)
            squares(1, x1, lambda k: (wo_read, 64), squares2)
            ht_write(1, tmp2, M_SH2)

            def hidden_hi(b, m, half):
                n = 2 * m + half
                act.wait_ge(u_done, b * 8 + (n + 1))
                act.wait_ge(u_read, b * 8 + (RING + n - 1))
                act.activation(relu[n % 2], pp[n % 4][:, :], ACT.Relu).then_inc(relu_done, 1)
                act.wait_ge(relu_done, b * 8 + (n + 1))
                act.activation(ou[:, 0, m, half * HALF:(half + 1) * HALF], relu[n % 2], ACT.Square).then_inc(u_hi, 1)

            def mlp_hi(b, j):
                pos = later_pos(16 + j)
                if j < 4:
                    act.wait_ge(y_done, (b - 1) * 16 + 4 * (j + 1))
                else:
                    act.wait_ge(u_done, b * 8 + 2 * (j - 3))
                split_hi(pos % STAGE_SLOTS, j % FLOW_SLOTS, b * 32 + arrived(pos))

            def mlp_block(b, last):
                for m in range(4):
                    for half in range(2):
                        hidden_hi(b, m, half)
                    mlp_hi(b, 4 + m)
                if not last:
                    for j in range(4):
                        mlp_hi(b + 1, j)

            with act.Fori(0, BLOCKS - 1) as b:
                mlp_block(b, False)
            mlp_block(BLOCKS - 1, True)

            act.wait_ge(y_read, 4 + 16 * BLOCKS)
            squares(2, x1, lambda k: (y_read, 4 + 16 * BLOCKS), squares2)

        @block.vector
        def _(dve):
            vec_ = nc.vector

            def split_lo(slot, split_slot, made):
                dve.wait_ge(hi_made, made)
                vec_.tensor_tensor(wsplit[:, split_slot, 1, :], stage[:, slot, :], wsplit[:, split_slot, 0, :].bitcast(F32),
                                   ALU.subtract).then_inc(taken, 1)

            def head_lo(h, j):
                split_lo(unit_pos(0, j) % STAGE_SLOTS, j % SPLIT_SLOTS, h * HEAD_UNITS + (j + 1))

            def ada_chunk(acc, place, arrivals):
                for k in range(KT):
                    pos, count = place(k), arrivals(k)
                    slot = count[0]
                    dve.wait_ge(staged[slot], count[1])
                    if k == 0:
                        vec_.tensor_scalar(acc, stage[:, slot, :], cond[:, 0:1], None, ALU.mult).then_inc(taken, 1)
                    else:
                        dve.wait_ge(taken, pos)
                        vec_.scalar_tensor_tensor(acc, stage[:, slot, :], cond[:, k:k + 1], acc,
                                                  ALU.mult, ALU.add).then_inc(taken, 1)

            def norm_scales(n, diag):
                dve.wait_ge(sq_read, KT * (n + 1))
                vec_.tensor_scalar(zcol[:, :], pa[2][:, 0:KT], 1.0 / D, EPS, ALU.mult, ALU.add).then_inc(z_done, 1)
                dve.wait_ge(pow_done, n + 1)
                d3 = diag.rearrange("p (a t) -> p a t", t=P)
                vec_.tensor_tensor(d3, ident[:, :].unsqueeze(1).to_broadcast([P, TT, P]),
                                   rcol[:, :].unsqueeze(2).to_broadcast([P, TT, P]), ALU.mult).then_inc(diag_done, 1)

            def ht_write(n, source, tmp, gain, shift):
                def lo(i):
                    half, k = divmod(i, KT)
                    part = slice(half * HALF, (half + 1) * HALF)
                    dve.wait_ge(ht_hi, 16 * n + i + 1)
                    vec_.scalar_tensor_tensor(ht[:, 1, k, part], tmp[i % 2], mods[:, shift + k:shift + k + 1],
                                              ht[:, 0, k, part].bitcast(F32), ALU.add, ALU.subtract).then_inc(ht_done, 1)
                for i in range(16):
                    half, k = divmod(i, KT)
                    if k == 0:
                        dve.wait_ge(bc_done, 2 * n + half + 1)
                    if i >= 2:
                        dve.wait_ge(ht_done, 16 * n + i - 1)
                    vec_.scalar_tensor_tensor(tmp[i % 2], source[:, k, half * HALF:(half + 1) * HALF],
                                              gains[:, gain, k:k + 1], pa[half][:, :], ALU.mult, ALU.mult).then_inc(scaled, 1)
                    if i >= 1:
                        lo(i - 1)
                lo(15)

            dve.wait_ge(cond_done, 1)
            for c in range(2):
                ada_chunk(ada_sum[c], lambda k: KT * c + k, lambda k: (k % 4, 16 * ((KT * c + k) // 4 + 1)))
            norm_scales(0, diag1)
            for c in range(2):
                dve.wait_ge(ada_done, c + 1)
                vec_.tensor_tensor(mods[:, 8 * c:8 * c + 8], pp[c][:, 0:8],
                                   vecs[:, C_ADAB + 8 * c:C_ADAB + 8 * c + 8], ALU.add).then_inc(mods_done, 1)
            dve.wait_ge(mods_done, 2)
            vec_.scalar_tensor_tensor(gains[:, 0, :], mods[:, M_SC1:M_SC1 + KT], 1.0, vecs[:, C_GMIX:C_GMIX + KT],
                                      ALU.add, ALU.mult).then_inc(gains_done, 1)
            dve.wait_ge(gains_done, 1)
            for j in range(2):
                split_lo(j, j, j + 1)
            ht_write(0, qkv, tmp1, 0, M_SH1)

            dve.wait_ge(trig_in, 16)
            with dve.Fori(0, HEADS) as h:
                for j in range(2, 6):
                    head_lo(h, j)
                for n in range(8):
                    m, half = divmod(n, 2)
                    part = slice(half * HALF, (half + 1) * HALF)
                    cos, sin = trig[:, 0, part], trig[:, 1, part]
                    psum = pp[n % 4][:, :]
                    dve.wait_ge(qk_done, h * 8 + (n + 1))
                    if m % 2 == 0:
                        vec_.tensor_tensor(qkv[:, m, part], psum, cos, ALU.mult)
                        vec_.tensor_tensor(qkv[:, m + 1, part], psum, sin, ALU.mult).then_inc(qk_read, 1)
                    else:
                        t1, t2 = rope_tmp[2 * half], rope_tmp[2 * half + 1]
                        vec_.tensor_tensor(t1, psum, sin, ALU.mult)
                        vec_.tensor_tensor(t2, psum, cos, ALU.mult).then_inc(qk_read, 1)
                        dve.wait_ge(qk_read, h * 8 + (n + 1))
                        vec_.tensor_tensor(qkv[:, m - 1, part], qkv[:, m - 1, part], t1, ALU.subtract)
                        vec_.tensor_tensor(qkv[:, m, part], qkv[:, m, part], t2, ALU.add).then_inc(roped, 1)
                    if half == 1:
                        head_lo(h, 6 + m)

                def count(k):
                    pos = head_pos(0, KT + k)
                    return pos % STAGE_SLOTS, h * (16 * HEAD_STREAM // STAGE_SLOTS) + 16 * (pos // STAGE_SLOTS + 1)
                ada_chunk(ada_sum[0], lambda k: head_pos(h, KT + k), count)
                dve.wait_ge(ada_done, h + 3)
                vec_.tensor_tensor(mods[:, bass.ds(h * 8 + 16, 8)], pa[2][:, 0:8],
                                   vecs[:, bass.ds(h * 8 + (C_ADAB + 16), 8)], ALU.add).then_inc(mods_done, 1)

                def scores(c):
                    dve.wait_ge(sc_done, h * NCHUNK + (c + 1))
                    vec_.tensor_tensor(sc[:, c % 2, :], pa[c % 2][:, 0:384], hc[:, H_MASK:H_MASK + 384], ALU.mult)\
                        .then_inc(sc_read, 1)

                def new_state(c):
                    dve.wait_ge(kv_done, h * 3 + (c + 1))
                    if c:
                        dve.wait_ge(state_done, h * 3 + c)
                    for a in range(2):
                        if c == 0:
                            last = vec_.tensor_copy(state[:, 0, a, :], pp[a][:, :])
                        else:
                            last = vec_.scalar_tensor_tensor(state[:, c % 2, a, :], state[:, (c - 1) % 2, a, :],
                                                             hc[:, H_DECAY:H_DECAY + 1], pp[a][:, :], ALU.mult, ALU.add)
                    last.then_inc(state_done, 1)

                def normalise(i):
                    dve.wait_ge(row_scale, h * TT + (i + 2))
                    vec_.tensor_scalar(og[:, i, :], pa[2 + i % 2][:, :], rs[:, 2, i % 2:i % 2 + 1], math.sqrt(DV),
                                       ALU.mult, ALU.mult)\
                        .then_inc(o_read, 1)

                dve.wait_ge(hc_in, h * 16 + 16)
                scores(0)
                scores(1)
                new_state(0)
                head_lo(h, 10)
                normalise(0)
                normalise(1)
                new_state(1)
                scores(2)
                head_lo(h, 11)
                normalise(2)
                normalise(3)
                new_state(2)
                scores(3)
                head_lo(h, 12)
                normalise(4)
                normalise(5)
                head_lo(h, 13)
                normalise(6)
                normalise(7)
                dve.wait_ge(o_read, h * TT + (2 + TT))
                for i in range(TT):
                    dve.wait_ge(silu_done, h * TT + (i + 1))
                    vec_.tensor_tensor(og[:, i, :], og[:, i, :], pp[i % 4][:, :], ALU.mult).then_inc(gated, 1)

            dve.wait_ge(mods_done, 6)
            vec_.tensor_scalar(gains[:, 1, :], mods[:, M_GT1:M_GT1 + KT], 1.0, None, ALU.add)
            vec_.tensor_scalar(gains[:, 2, :], mods[:, M_GT2:M_GT2 + KT], 1.0, None, ALU.add)
            vec_.scalar_tensor_tensor(gains[:, 3, :], mods[:, M_SC2:M_SC2 + KT], 1.0, vecs[:, C_GMLP:C_GMLP + KT],
                                      ALU.add, ALU.mult).then_inc(gains_done, 1)
            dve.wait_ge(gains_done, 2)

            def o_split_lo(n):
                h, c = divmod(n, 4)
                dve.wait_ge(o_hi, n + 1)
                hi, lo = ((ht[:, 0, 4:8, :], ht[:, 1, 4:8, :]) if h % 2 == 0 else (ou[:, 0, :, :], ou[:, 1, :, :]))
                dst = lo[:, :, c * 256:(c + 1) * 256].rearrange("p d (a t) -> p d a t", a=2)
                src = hi[:, :, c * 256:(c + 1) * 256].rearrange("p d (a t) -> p d a t", a=2).bitcast(F32)
                vec_.tensor_tensor(dst, ostage[:, n % 2, :, :].rearrange("p a (d t) -> p d a t", d=4), src, ALU.subtract)\
                    .then_inc(o_taken, 1)

            def later_lo(i):
                split_lo(later_pos(i) % STAGE_SLOTS, i % FLOW_SLOTS, W_OUT0 + i + 1)

            for n in range(4):
                o_split_lo(n)
            later_lo(2)
            later_lo(3)
            for n in range(4, 8):
                o_split_lo(n)
            dve.wait_ge(x1_in, 16 * KT)
            for h in range(HEADS):
                for j in range(4):
                    for g in range(4 * j, 4 * j + 4):
                        m, half = divmod(g, 2)
                        part = slice(half * HALF, (half + 1) * HALF)
                        dve.wait_ge(wo_done, 16 * h + g + 1)
                        vec_.scalar_tensor_tensor(x1[:, m, part], pp[g % 4][:, :], gains[:, 1, m:m + 1], x1[:, m, part],
                                                  ALU.mult, ALU.add).then_inc(wo_read, 1)
                    later_lo(4 * h + 4 + j)
                    if j == 3 and h < 2:
                        for n in range(4 * h + 8, 4 * h + 12):
                            o_split_lo(n)

            norm_scales(1, diag2)
            ht_write(1, x1, tmp2, 3, M_SH2)

            def hidden_lo(b, m, half):
                n = 2 * m + half
                psum = pp[n % 4][:, :]
                part = slice(half * HALF, (half + 1) * HALF)
                dve.wait_ge(relu_done, b * 8 + (n + 1))
                vec_.scalar_tensor_tensor(psum, psum, 0.0, relu[n % 2], ALU.max, ALU.mult).then_inc(u_sq, 1)
                dve.wait_ge(u_hi, b * 8 + (n + 1))
                dve.wait_ge(u_sq, b * 8 + (n + 1))
                vec_.tensor_tensor(ou[:, 1, m, part], psum, ou[:, 0, m, part].bitcast(F32), ALU.subtract).then_inc(u_read, 1)

            def mlp_lo(b, j):
                split_lo(later_pos(16 + j) % STAGE_SLOTS, j % FLOW_SLOTS, b * 8 + (W_MLP0 + j + 1))

            def mlp_block(b, last):
                for m in range(4):
                    for half in range(2):
                        hidden_lo(b, m, half)
                    mlp_lo(b, 4 + m)
                for j in range(4):
                    for g in range(4 * j, 4 * j + 4):
                        m, half = divmod(g, 2)
                        part = slice(half * HALF, (half + 1) * HALF)
                        dve.wait_ge(y_done, b * 16 + (g + 1))
                        vec_.scalar_tensor_tensor(x1[:, m, part], pa[g % 4][:, :], gains[:, 2, m:m + 1], x1[:, m, part],
                                                  ALU.mult, ALU.add).then_inc(y_read, 1)
                    if not last:
                        mlp_lo(b + 1, j)

            with dve.Fori(0, BLOCKS - 1) as b:
                mlp_block(b, False)
            mlp_block(BLOCKS - 1, True)

            norm_scales(2, diag2)
            for n in range(16):
                half, k = divmod(n, KT)
                if k == 0:
                    dve.wait_ge(bc_done, 4 + half + 1)
                if n >= 4:
                    dve.wait_ge(out_stored[n % 4], 16 * (n // 4))
                vec_.scalar_tensor_tensor(tmp2[n % 4], x1[:, k, half * HALF:(half + 1) * HALF],
                                          vecs[:, C_GFIN + k:C_GFIN + k + 1], pa[half][:, :], ALU.mult, ALU.mult)\
                    .then_inc(out_ready, 1)

        @block.tensor
        def _(pe):
            mm = nc.tensor.matmul

            def product(out, stationary, moving, start, stop):
                mm(out, stationary(0), moving(0), start=start, stop=False)
                mm(out, stationary(0), moving(1), start=False, stop=False)
                return mm(out, stationary(1), moving(0), start=False, stop=stop)

            def by_feature(slot, tile):
                return lambda part: wsplit[:, slot, part, tile * P:(tile + 1) * P]

            def half_of(x, k, half):
                return lambda part: x[:, part, k, half * HALF:(half + 1) * HALF]

            def token_sums(n, k, sq):
                pe.wait_ge(squared, KT * n + k + 1)
                for j in range(TT):
                    last = mm(pa[2][:, j:j + 1], sq[k % 2][:, j * P:(j + 1) * P], ones[:, 0:1],
                              start=(k == 0 and j == 0), stop=(k == KT - 1), skip_group_check=True)
                last.then_inc(sq_read, 1)

            def broadcast(n, diag):
                pe.wait_ge(diag_done, n + 1)
                for half in range(2):
                    mm(pa[half][:, :], ones[:, :], diag[:, half * HALF:(half + 1) * HALF], start=True, stop=True)\
                        .then_inc(bc_done, 1)

            def ada_total(bank, column, acc):
                for m in range(KT):
                    last = mm(bank[:, column + m:column + m + 1], acc[:, m * P:(m + 1) * P], ones[:, 0:1],
                              start=True, stop=True)
                last.then_inc(ada_done, 1)

            pe.sem_inc(g_unit_free, 3)
            pe.sem_inc(g_done, RING)
            pe.sem_inc(gated, RING)
            pe.sem_inc(o_squared, RING)
            pe.sem_inc(o_read, 2)
            pe.sem_inc(t_read, RING)
            pe.sem_inc(row_scale, 1)
            pe.sem_inc(stored[0], 16)
            pe.sem_inc(stored[1], 16)
            pe.sem_inc(u_read, RING)
            pe.sem_inc(y_read, 4)

            pe.wait_ge(setup_done, 2)
            for k in range(KT):
                token_sums(0, k, squares1)
            pe.wait_ge(taken, KT)
            ada_total(pp[0], 0, ada_sum[0])
            pe.wait_ge(consts_in, 32)
            broadcast(0, diag1)
            pe.wait_ge(taken, 2 * KT)
            ada_total(pp[1], 0, ada_sum[1])

            with pe.Fori(0, HEADS) as h:
                for m in range(4):
                    pe.wait_ge(taken, unit_pos(h, m) + 1)
                    for half in range(2):
                        n = 2 * m + half
                        if n < 4:
                            pe.wait_ge(gated, h * TT + (5 + n))
                        else:
                            pe.wait_ge(qk_read, h * TT + (n - 3))
                        for k in range(KT):
                            if m == 0:
                                pe.wait_ge(ht_done, 8 * half + k + 1)
                            last = product(pp[n % 4][:, :], by_feature(m, k), half_of(ht, k, half), k == 0, k == KT - 1)
                        last.then_inc(qk_done, 1)

                def token_panel(i, first_unit, free):
                    for k in range(KT):
                        u, slot = divmod(k, 2)[0], (first_unit + k // 2) % SPLIT_SLOTS
                        last = product(pp[i % 4][:, :], lambda part: ht[:, part, k, i * P:(i + 1) * P],
                                       lambda part: wsplit[:, slot, part, (k % 2) * DV:(k % 2 + 1) * DV], k == 0, k == KT - 1)
                        if i == TT - 1 and k in (1, 3, 5):
                            last.then_inc(free, 1)
                    return last

                for i in range(TT):
                    if i == 0:
                        pe.wait_ge(taken, unit_pos(h, 7) + 1)
                    if i < 4:
                        pe.wait_ge(qk_read, h * TT + (5 + i))
                    else:
                        pe.wait_ge(v_read, h * TT + (i - 3))
                    token_panel(i, 4, v_unit_free).then_inc(v_done, 1)

                pe.wait_ge(o_read, h * TT + 2)
                pe.wait_ge(taken, head_pos(h, KT + KT - 1) + 1)
                ada_total(pa[2], 0, ada_sum[0])

                def scores(c):
                    if c < 2:
                        pe.wait_ge(t_read, h * TT + RING)
                    else:
                        pe.wait_ge(sc_read, h * NCHUNK + (c - 1))
                    t0 = c * CHUNK
                    for a in range(2):
                        mm(pa[c % 2][:, 0:256], qkv[:, 2 + a, t0:t0 + P], qkv[:, a, t0:t0 + 256], start=a == 0, stop=a == 1)
                    for a in range(2):
                        last = mm(pa[c % 2][:, 256:384], qkv[:, 2 + a, t0 + P:t0 + 256], qkv[:, a, t0 + P:t0 + 256],
                                  start=a == 0, stop=a == 1)
                    last.then_inc(sc_done, 1)

                def keys(c):
                    if c < 2:
                        pe.wait_ge(v_read, h * TT + (7 + c))
                    else:
                        pe.wait_ge(kt_read, h * 3 + 1)
                    for s in range(2):
                        for a in range(2):
                            col = s * DK + a * P
                            t0 = c * CHUNK + s * P
                            last = nc.tensor.transpose(pp[2 + c % 2][:, col:col + P], qkv[:, 2 + a, t0:t0 + P], ident[:, :])
                    last.then_inc(kt_done, 1)

                def keys_values(c):
                    if c == 0:
                        pe.wait_ge(v_read, h * TT + TT)
                    else:
                        pe.wait_ge(state_done, h * 3 + c)
                    pe.wait_ge(kt_read, h * 3 + (c + 1))
                    for a in range(2):
                        for s in range(2):
                            last = mm(pp[a][:, :], kn[:, c % 2, s, a * P:(a + 1) * P], v[:, 2 * c + s, :],
                                      start=s == 0, stop=s == 1)
                    last.then_inc(kv_done, 1)

                def outputs(i):
                    c, par = divmod(i, 2)
                    pe.wait_ge(o_read, h * TT + (i + 1))
                    if i == 0:
                        pe.wait_ge(mods_done, h + 3)
                    pe.wait_ge(sc_read, h * NCHUNK + (c + 1))
                    bank = pa[2 + par][:, :]
                    pairs = [(sc[:, c % 2, (s + par) * P:(s + par + 1) * P], v[:, 2 * c + s, :]) for s in range(par + 1)]
                    if c:
                        pe.wait_ge(state_done, h * 3 + c)
                        pairs += [(qkv[:, a, i * P:(i + 1) * P], state[:, (c - 1) % 2, a, :]) for a in range(2)]
                    for n, (stationary, moving) in enumerate(pairs):
                        last = mm(bank, stationary, moving, start=n == 0, stop=n == len(pairs) - 1)
                    last.then_inc(o_done, 1)

                pe.wait_ge(roped, h * 4 + 4)
                scores(0)
                keys(0)
                scores(1)
                keys(1)
                keys_values(0)
                outputs(0)
                outputs(1)
                keys_values(1)
                scores(2)
                keys(2)
                outputs(2)
                outputs(3)
                keys_values(2)
                scores(3)
                for i in range(4, 8):
                    outputs(i)

                def turn(i):
                    if i < 2:
                        pe.wait_ge(sc_read, h * NCHUNK + (3 + i))
                    else:
                        pe.wait_ge(t_read, h * TT + (RING + i - 1))
                    pe.wait_ge(gated, h * TT + (RING + i + 1))
                    for d in range(4):
                        last = nc.tensor.transpose(pa[i % 2][:, d * P:(d + 1) * P], og[:, i, d * P:(d + 1) * P], ident[:, :])
                    last.then_inc(t_done, 1)

                pe.wait_ge(taken, unit_pos(h, 11) + 1)
                pe.wait_ge(state_done, h * 3 + 3)
                pe.wait_ge(kt_read, h * 3 + 3)
                for i in range(TT):
                    if i >= 4:
                        pe.wait_ge(gated, h * TT + (RING + i - 3))
                    token_panel(i, 8, g_unit_free).then_inc(g_done, 1)
                    if i:
                        turn(i - 1)
                turn(TT - 1)

            for h in range(HEADS):
                src = ht[:, :, 4:8, :] if h % 2 == 0 else ou[:, :, :, :]
                for g in range(16):
                    m, half = divmod(g, 2)
                    if h == 0 and g < 4:
                        pe.wait_ge(gated, TT * HEADS + 5 + g)
                    else:
                        pe.wait_ge(wo_read, 16 * h + g - 3)
                    if g < 2:
                        pe.wait_ge(o_taken, 4 * h + 2 * (half + 1))
                    if g % 4 == 0:
                        pe.wait_ge(taken, later_pos(4 * h + g // 4) + 1)
                    for k in range(4):
                        last = product(pp[g % 4][:, :], by_feature(m // 2, (m % 2) * 4 + k), half_of(src, k, half), k == 0, k == 3)
                    last.then_inc(wo_done, 1)

            for k in range(KT):
                token_sums(1, k, squares2)
            broadcast(1, diag2)

            pe.wait_ge(wo_read, 64)

            def hidden(b, m, half, waits):
                n = 2 * m + half
                if half == 0:
                    pe.wait_ge(taken, b * 8 + (later_pos(16 + m) + 1))
                pe.wait_ge(u_read, b * 8 + (RING + n - 3))
                for k in range(KT):
                    if m == 0:
                        pe.wait_ge(ht_done, 16 + 8 * half + k + 1)
                    last = product(pp[n % 4][:, :], by_feature(m, k), half_of(ht, k, half), k == 0, k == KT - 1)
                last.then_inc(u_done, 1)

            def second(b, g, ks):
                m, half = divmod(g, 2)
                for k in ks:
                    if g < 2:
                        pe.wait_ge(u_read, b * 8 + (RING + 2 * k + half + 1))
                    last = product(pa[g % 4][:, :], by_feature(m // 2, (m % 2) * 4 + k), half_of(ou, k, half), k == 0, k == 3)
                return last

            def mlp_block(b):
                for m in range(4):
                    for half in range(2):
                        hidden(b, m, half, True)
                for g in range(16):
                    if g % 4 == 0:
                        pe.wait_ge(taken, b * 8 + (later_pos(16 + 4 + g // 4) + 1))
                    pe.wait_ge(y_read, b * 16 + (g + 1))
                    if g < 4:
                        second(b, g, range(3))
                        if g == 3:
                            for g2 in range(4):
                                second(b, g2, [3]).then_inc(y_done, 1)
                    else:
                        second(b, g, range(4)).then_inc(y_done, 1)

            with pe.Fori(0, BLOCKS) as b:
                mlp_block(b)

            pe.wait_ge(y_read, 4 + 16 * BLOCKS)
            for k in range(KT):
                token_sums(2, k, squares2)
            broadcast(2, diag2)



def kernel(**inputs):
    import numpy as _np
    import concourse.bacc as _bacc
    from concourse import mybir as _mybir
    from concourse.bass_utils import run_bass_kernel_spmd as _run

    f = {k: _np.asarray(a) for k, a in inputs.items()}

    def columns(a):
        return a.reshape(-1, P).T

    def rows(a):
        return a.reshape(-1, P, a.shape[-1])

    w_in = f["ret_w_in"][0]
    q, k, val, gate = (w_in[:, a:b] for a, b in ((0, D), (D, 2 * D), (2 * D, 4 * D), (4 * D, 6 * D)))
    units = []
    for h in range(HEADS):
        for m in (q, k):
            part = rows(m)[:, :, h * DK:(h + 1) * DK]
            for odd in range(2):
                units.append(part[:, :, odd::2].transpose(1, 0, 2).reshape(P, UNIT))
        for m in (val, gate):
            part = rows(m)[:, :, h * DV:(h + 1) * DV]
            for j in range(4):
                units.append(part[2 * j:2 * j + 2].transpose(1, 0, 2).reshape(P, UNIT))

    def panel(w):
        r = w.reshape(4, P, 4, 2, P).transpose(2, 1, 3, 0, 4)
        return [r[j].reshape(P, UNIT) for j in range(4)]

    for h in range(HEADS):
        units += panel(f["ret_w_out"][0][h * DV:(h + 1) * DV])
    for b in range(BLOCKS):
        w1 = rows(f["mlp_w1"][0])[:, :, b * HALF:(b + 1) * HALF]
        units += [w1[:, :, m * P:(m + 1) * P].transpose(1, 0, 2).reshape(P, UNIT) for m in range(4)]
        units += panel(f["mlp_w2"][0][b * HALF:(b + 1) * HALF])

    vec = _np.concatenate([columns(a) for a in (f["c"][0], f["ada_b"][0], f["norm_mix_g"][0], f["norm_mlp_g"][0],
                                                f["final_norm_g"])], axis=1)
    rope, heads, eye = constants()
    arrays = {
        "xT": f["x"][0].T.reshape(KT, P, T),
        "vec": vec,
        "ada": f["ada_w"][0].reshape(KT, P, 6, D).transpose(2, 0, 1, 3),
        "weights": _np.stack(units),
        "rope": rope, "heads": heads, "eye": eye,
    }
    arrays = {name: _np.ascontiguousarray(a) for name, a in arrays.items()}
    nc = _bacc.Bacc("TRN2", target_bir_lowering=False, num_devices=1)
    args = [nc.dram_tensor(name, a.shape, _mybir.dt.from_np(a.dtype), kind="ExternalInput").ap() for name, a in arrays.items()]
    out = nc.dram_tensor("outT", (KT, P, T), _mybir.dt.float32, kind="ExternalOutput").ap()
    build(nc, *args, out)
    r = _run(nc, [arrays], core_ids=[0])
    return r.results[0]["outT"].reshape(D, T).T.reshape(1, T, D)
```

```python
import math
from contextlib import ExitStack

import numpy as np
import concourse.bass as bass
from concourse import mybir

F32 = mybir.dt.float32
F32R = mybir.dt.float32r
ALU = mybir.AluOpType
ACT = mybir.ActivationFunctionType

P = 128
D = 1024
T = 1024
KT = D // P
HALF = 512
HEADS = 4
DK = D // HEADS
DV = 2 * D // HEADS
FF = 4 * D
CHUNK = 256
NCHUNK = T // CHUNK
TT = T // P
UNIT = 1024
STAGE_SLOTS = 4
SPLIT_SLOTS = 6
FLOW_SLOTS = 4
BLOCKS = FF // HALF
EPS = 1e-6

C_COND, C_ADAB, C_GMIX, C_GMLP, C_GFIN, N_VEC = 0, 8, 56, 64, 72, 80
H_MASK, H_EPS, H_ZETA, H_DECAY, N_HEAD = 0, 384, 386, 388, 390
M_SH1, M_SC1, M_GT1, M_SH2, M_SC2, M_GT2 = range(0, 48, 8)

ADA_FIRST = 2 * KT
HEAD_UNITS = 12
HEAD_STREAM = HEAD_UNITS + KT
START = [("a", 1, k) for k in range(KT)] + [("w", 0, 0)] + [("a", 0, k) for k in range(KT)] + [("w", 1, 0)]
STREAM = [("w", j) for j in range(2, 10)] + [("a", k) for k in range(KT)] + [("w", j) for j in range(10, 14)]
W_OUT0 = HEADS * HEAD_UNITS
W_MLP0 = W_OUT0 + 4 * HEADS


def constants():
    inv = np.float32(10000.0) ** (-np.linspace(0.0, 1.0, DK // 2, dtype=np.float32))
    ang = (np.arange(T, dtype=np.float32)[:, None] * inv[None, :].astype(np.float32)).astype(np.float32)
    rope = np.stack([np.cos(ang).T, np.sin(ang).T], axis=1).astype(np.float32)
    lg = np.log1p(-np.exp2(-5.0 - np.arange(HEADS)))
    s = np.arange(P)[:, None]
    t = np.arange(P)[None, :]
    tri = (s <= t).astype(np.float64)
    k_scale = DK ** -0.5
    heads = np.zeros((HEADS, P, N_HEAD))
    for h in range(HEADS):
        down = np.exp(-(s + 1.0) * lg[h]) * k_scale
        heads[h, :, 0:128] = tri * down
        heads[h, :, 128:256] = down
        heads[h, :, 256:384] = tri * np.exp(-(s + 129.0) * lg[h]) * k_scale
        for a in range(2):
            xi = np.exp((s[:, 0] + 128 * a + 1.0) * lg[h])
            heads[h, :, H_EPS + a] = DV * EPS / (xi * xi)
            heads[h, :, H_ZETA + a] = np.exp((CHUNK - 1.0 - 128 * a - s[:, 0]) * lg[h]) * k_scale
        heads[h, :, H_DECAY] = np.exp(CHUNK * lg[h])
    return rope, heads.astype(np.float32), np.eye(P, dtype=np.float32)


def build(nc, xT, vec, ada, weights, rope, heads, eye, outT):
    ctx = ExitStack()
    with ctx:
        def sem(name):
            return ctx.enter_context(nc.semaphore(name))

        def sb(name, shape, dt=F32, into=ctx):
            return into.enter_context(nc.sbuf_tensor(name, shape, dt))

        ht = sb("ht", [P, 2, KT, T], F32R)
        stage = sb("stage", [P, STAGE_SLOTS, UNIT])
        wsplit = sb("wsplit", [P, SPLIT_SLOTS, 2, UNIT], F32R)
        vecs = sb("vecs", [P, N_VEC])
        mods = sb("mods", [P, 48])
        gains = sb("gains", [P, 4, KT])
        cond = sb("cond", [P, KT])
        ident = sb("ident", [P, P])
        ones = sb("ones", [P, P])
        power = sb("power", [P, KT])
        zcol = sb("zcol", [P, KT])
        rcol = sb("rcol", [P, KT])

        first = ExitStack()
        qkv = sb("qkv", [P, 8, T], into=first)
        og = sb("og", [P, TT, DV], into=first)
        trig = sb("trig", [P, 2, T], into=first)
        turned = sb("turned", [P, 2, DV], into=first)
        hc = sb("hc", [P, N_HEAD], into=first)
        rs = sb("rs", [P, 3, 2], into=first)
        sc = sb("sc", [P, 2, 384], into=first)
        kn = sb("kn", [P, 2, 2, DK], into=first)
        state = sb("state", [P, 2, 2, DV], into=first)
        first.close()
        v = qkv[:, 4:8, :].rearrange("p a (b n) -> p (a b) n", n=DV)
        ogf = og[:, :, :].rearrange("p a n -> p (a n)")
        ada_sum = ogf[:, 0:UNIT]
        squares1 = [ogf[:, (2 + i) * UNIT:(3 + i) * UNIT] for i in range(2)]
        sums1 = ogf[:, UNIT:2 * UNIT]
        rope_tmp = [ogf[:, 2048 + i * HALF:2048 + (i + 1) * HALF] for i in range(4)]
        statef = state[:, :, :, :].rearrange("p a b n -> p (a b n)")
        diag1 = statef[:, 0:UNIT]
        rms_half = statef[:, UNIT:UNIT + HALF]

        later = ExitStack()
        ou = sb("ou", [P, 2, 4, T], F32R, into=later)
        x1 = sb("x1", [P, KT, T], into=later)
        ostage = sb("ostage", [P, 2, 2, DV], into=later)
        spare = sb("spare", [P, 2, HALF], into=later)
        later.close()
        rows4 = ostage[:, :, :, :].rearrange("p a b n -> p (a b) n")
        squares2 = [rows4[:, i] for i in range(2)]
        scaled2 = [rows4[:, 2 + i] for i in range(2)]
        outs = [rows4[:, i] for i in range(4)]
        relu = [spare[:, i] for i in range(2)]
        sums = [spare[:, i] for i in range(2)]

        pp = [ctx.enter_context(nc.psum_tensor(f"pp{i}", [P, HALF], F32)) for i in range(4)]
        pa = [ctx.enter_context(nc.psum_tensor(f"pa{i}", [P, HALF], F32)) for i in range(4)]

        gated_dram = nc.dram_tensor("gated_T", (HEADS, TT, P, DV), F32, kind="Internal").ap()

        consts_in, trig_in = sem("consts_in"), sem("trig_in")
        x_in = [sem(f"x_in{k}") for k in range(KT)]
        staged = [sem(f"staged{i}") for i in range(STAGE_SLOTS)]
        taken = sem("taken")
        hi_made = sem("hi_made")
        setup_done = sem("setup_done")
        cond_done = sem("cond_done")
        ada_done = sem("ada_done")
        mods_done = sem("mods_done")
        gains_done = sem("gains_done")
        squared = sem("squared")
        sq_added = sem("sq_added")
        sums_done = sem("sums_done")
        z_done, pow_done, diag_done, bc_done = sem("z_done"), sem("pow_done"), sem("diag_done"), sem("bc_done")
        scaled, ht_hi, ht_done = sem("scaled"), sem("ht_hi"), sem("ht_done")
        gained = sem("gained")
        rms_copied = sem("rms_copied")
        scaled_2 = sem("scaled_2")
        qk_done, qk_read, roped = sem("qk_done"), sem("qk_read"), sem("roped")
        v_done, v_read, v_unit_free = sem("v_done"), sem("v_read"), sem("v_unit_free")
        sc_done, sc_read = sem("sc_done"), sem("sc_read")
        kt_done, kt_read = sem("kt_done"), sem("kt_read")
        kv_done, state_done = sem("kv_done"), sem("state_done")
        o_done, o_squared, row_scale, o_read = sem("o_done"), sem("o_squared"), sem("row_scale"), sem("o_read")
        scale_step = sem("scale_step")
        g_done, silu_done, gated, g_unit_free = sem("g_done"), sem("silu_done"), sem("gated"), sem("g_unit_free")
        t_done, t_read = sem("t_done"), sem("t_read")
        hc_in = sem("hc_in")
        stored = [sem("stored0"), sem("stored1")]
        o_in = [sem("o_in0"), sem("o_in1")]
        o_hi, o_taken = sem("o_hi"), sem("o_taken")
        wo_done, wo_read = sem("wo_done"), sem("wo_read")
        u_done, relu_done, u_sq, u_hi, u_read = sem("u_done"), sem("relu_done"), sem("u_sq"), sem("u_hi"), sem("u_read")
        y_done, y_read = sem("y_done"), sem("y_read")
        out_ready = sem("out_ready")
        out_stored = [sem(f"out_stored{i}") for i in range(4)]

        RING = 8

        block = ctx.enter_context(nc.Block())

        def head_pos(h, idx):
            return h * HEAD_STREAM + ADA_FIRST + 2 + idx

        def unit_pos(h, j):
            return h * HEAD_STREAM + ADA_FIRST + j + (KT if j in (10, 11, 12, 13) else 0)

        def out_slot(n):
            slots = [2 + i % 2 if i < KT else i % 4 for i in range(16)]
            return slots[n], slots[:n].count(slots[n])

        def panel_half(h, k, half):
            if h % 2 == 0:
                return lambda part: ou[:, part, k, half * HALF:(half + 1) * HALF]
            return lambda part: ht[:, part, 2 * k + half, HALF:T]

        def panel_part(h, part, c):
            if h % 2 == 0:
                x = ou[:, part, :, c * 256:(c + 1) * 256]
            else:
                at = HALF + (c % 2) * 256
                x = ht[:, part, c // 2::2, at:at + 256]
            return x.rearrange("p d (a t) -> p d a t", a=2)

        def later_pos(i):
            return i + ADA_FIRST + HEADS * HEAD_STREAM

        @block.sync
        def _(sp):
            def load(source, slot, p):
                sp.wait_ge(taken, p - STAGE_SLOTS + 1)
                sp.dma_start(stage[:, slot, :], source).then_inc(staged[slot], 16)

            sp.dma_start(vecs[:, :], vec).then_inc(consts_in, 16)
            sp.dma_start(ident[:, :], eye).then_inc(consts_in, 16)
            for p, (kind, a, b) in enumerate(START):
                if p == KT:
                    for k in range(KT):
                        sp.dma_start(qkv[:, k, :], xT[k]).then_inc(x_in[k], 16)
                source = weights[a] if kind == "w" else ada[a, b]
                if p < STAGE_SLOTS:
                    sp.dma_start(stage[:, p, :], source).then_inc(staged[p], 16)
                else:
                    load(source, p % STAGE_SLOTS, p)
            sp.dma_start(trig[:, :, :], rope).then_inc(trig_in, 16)
            with sp.Fori(0, HEADS) as h:
                for idx, (kind, j) in enumerate(STREAM):
                    if idx == KT:
                        sp.wait_ge(row_scale, h * TT + 1)
                        sp.dma_start(hc[:, :], heads[h]).then_inc(hc_in, 16)
                    slot = (2 + idx) % STAGE_SLOTS
                    source = weights[h * HEAD_UNITS + j] if kind == "w" else ada[h + 2, j]
                    load(source, slot, head_pos(h, idx))
            for i in range(2, 16):
                if i == 4:
                    for a in range(2):
                        sp.wait_ge(stored[a], 16 * (1 + 4 * HEADS))
                    for k in range(KT):
                        sp.dma_start(x1[:, k, :], xT[k]).then_inc(x_in[k], 16)
                load(weights[W_OUT0 + i], i % STAGE_SLOTS, later_pos(i))
            for j in range(8):
                load(weights[W_MLP0 + j], j % STAGE_SLOTS, later_pos(16 + j))
            with sp.Fori(1, BLOCKS) as b:
                for j in range(8):
                    load(weights[b * 8 + (W_MLP0 + j)], j % STAGE_SLOTS, b * 8 + later_pos(16 + j))
            for n in range(16):
                half, k = divmod(n, KT)
                slot, use = out_slot(n)
                sp.wait_ge(out_ready, n + 1)
                sp.dma_start(outT[k][:, half * HALF:(half + 1) * HALF], outs[slot]).then_inc(out_stored[slot], 16)
            for slot in range(4):
                sp.wait_ge(out_stored[slot], 16 * sum(out_slot(n)[0] == slot for n in range(16)))

        @block.gpsimd
        def _(pool):
            pool.memset(power[:, :], -0.5).then_inc(setup_done, 1)
            pool.memset(ones[:, :], 1.0).then_inc(setup_done, 1)
            pool.wait_ge(setup_done, 2)

            def norm_power(n, cols):
                pool.wait_ge(z_done, n)
                pool.tensor_tensor(rcol[:, cols], zcol[:, cols], power[:, cols], ALU.pow).then_inc(pow_done, 1)

            norm_power(1, slice(0, KT))
            pool.wait_ge(rms_copied, 1)
            for k in range(KT):
                x_part = qkv[:, k, HALF:T]
                pool.wait_ge(gained, k + 1)
                pool.tensor_tensor(x_part, x_part, rms_half, ALU.mult).then_inc(scaled_2, 1)
            with pool.Fori(0, HEADS) as h:
                for i in range(TT):
                    a = i % 2
                    pool.wait_ge(o_squared, h * TT + (RING + i + 1))
                    if i == 0:
                        pool.wait_ge(hc_in, h * 16 + 16)
                    pool.tensor_tensor(rs[:, 1, a:a + 1], rs[:, 0, a:a + 1], hc[:, H_EPS + a:H_EPS + a + 1], ALU.add)\
                        .then_inc(scale_step, 1)
                    pool.wait_ge(scale_step, h * TT + (i + 1))
                    pool.tensor_tensor(rs[:, 2, a:a + 1], rs[:, 1, a:a + 1], power[:, 0:1], ALU.pow).then_inc(row_scale, 1)
            for h in range(HEADS):
                for a in range(2):
                    pool.wait_ge(stored[a], 16 * (1 + 4 * (h + 1)))
                if h == 0:
                    pool.wait_ge(o_squared, RING + TT * HEADS)
                for c in range(4):
                    n = 4 * h + c
                    if n >= 2:
                        pool.wait_ge(o_taken, n - 1)
                    pool.dma_start(ostage[:, n % 2, :, :], gated_dram[h, 2 * c:2 * c + 2].rearrange("a p n -> p a n"))\
                        .then_inc(o_in[n % 2], 16)

            def add_square(n):
                half, m = divmod(n % 16, KT)
                pool.wait_ge(squared, KT + n + 1)
                if m == 0:
                    pool.tensor_copy(sums[half], squares2[n % 2]).then_inc(sq_added, 1)
                else:
                    pool.wait_ge(sq_added, KT + n)
                    pool.tensor_tensor(sums[half], sums[half], squares2[n % 2], ALU.add).then_inc(sq_added, 1)

            for norm in range(2):
                for n in range(16):
                    add_square(16 * norm + n)
                    if n == KT:
                        norm_power(2 + 2 * norm, slice(0, 4))
                norm_power(3 + 2 * norm, slice(4, 8))

        @block.scalar
        def _(act):
            def split_hi(slot, split_slot, arrived):
                act.wait_ge(staged[slot], arrived)
                act.activation(wsplit[:, split_slot, 0, :], stage[:, slot, :], ACT.Copy).then_inc(hi_made, 1)

            def arrived(pos0):
                return 16 * (pos0 // STAGE_SLOTS + 1)

            def head_hi(h, j):
                if j in (2, 3, 4):
                    act.wait_ge(g_unit_free, h * 3 + (j - 1))
                elif j == 5:
                    act.wait_ge(g_done, h * TT + RING)
                elif j in (6, 7, 8, 9):
                    act.wait_ge(qk_done, h * TT + 2 * (j - 5))
                elif j in (10, 11, 12):
                    act.wait_ge(v_unit_free, h * 3 + (j - 9))
                else:
                    act.wait_ge(v_done, h * TT + TT)
                pos = unit_pos(0, j)
                split_hi(pos % STAGE_SLOTS, j % SPLIT_SLOTS, h * (16 * HEAD_STREAM // STAGE_SLOTS) + arrived(pos))

            def square_half(n, count):
                half, m = divmod(n % 16, KT)
                act.wait_ge(*count)
                if n >= 2:
                    act.wait_ge(sq_added, KT + n - 1)
                act.activation(squares2[n % 2], x1[:, m, half * HALF:(half + 1) * HALF], ACT.Square).then_inc(squared, 1)

            def ht_write(n, source, shift, ready):
                half, k = divmod(n % 16, KT)
                act.wait_ge(*ready)
                act.activation(ht[:, 0, k, half * HALF:(half + 1) * HALF], source, ACT.Identity,
                               bias=mods[:, shift + k:shift + k + 1]).then_inc(ht_hi, 1)

            act.wait_ge(consts_in, 32)
            act.activation(cond[:, :], vecs[:, C_COND:C_COND + KT], ACT.Silu).then_inc(cond_done, 1)
            for k in range(KT):
                act.wait_ge(x_in[k], 16)
                if k >= 2:
                    act.wait_ge(sq_added, k - 1)
                act.activation(squares1[k % 2], qkv[:, k, :], ACT.Square).then_inc(squared, 1)
            split_hi(0, 0, arrived(KT))
            act.wait_ge(gains_done, 1)
            for k in range(KT):
                act.activation(qkv[:, k, HALF:T], qkv[:, k, HALF:T], ACT.Copy, scale=gains[:, 0, k:k + 1]).then_inc(gained, 1)
            act.wait_ge(bc_done, 2)
            act.activation(rms_half, pa[1][:, :], ACT.Copy).then_inc(rms_copied, 1)
            act.wait_ge(mods_done, 2)
            for n in range(16):
                half, k = divmod(n, KT)
                ht_write(n, qkv[:, k, half * HALF:(half + 1) * HALF], M_SH1,
                         (scaled_2, k + 1) if half else (scaled, k + 1))
                if n == KT:
                    split_hi(1, 1, arrived(ADA_FIRST + 1))

            def head(h, last):
                for j in range(2, 10):
                    head_hi(h, j)
                for i in range(TT):
                    act.wait_ge(v_done, h * TT + (i + 1))
                    act.activation(v[:, i, :], pp[i % 4][:, :], ACT.Copy).then_inc(v_read, 1)

                def keys(c):
                    act.wait_ge(kt_done, h * 3 + (c + 1))
                    for a in range(2):
                        last = act.activation(kn[:, c % 2, a, :], pp[2 + c % 2][:, a * DK:(a + 1) * DK], ACT.Copy,
                                              scale=hc[:, H_ZETA + a:H_ZETA + a + 1])
                    last.then_inc(kt_read, 1)

                def square(i):
                    act.wait_ge(o_done, h * TT + (i + 1))
                    act.activation(og[:, i, :], pa[2 + i % 2][:, :], ACT.Square, accum_out=rs[:, 0, i % 2:i % 2 + 1])\
                        .then_inc(o_squared, 1)

                act.wait_ge(hc_in, h * 16 + 16)
                keys(0)
                keys(1)
                head_hi(h, 10)
                square(0)
                square(1)
                keys(2)
                head_hi(h, 11)
                square(2)
                square(3)
                head_hi(h, 12)
                square(4)
                square(5)
                head_hi(h, 13)
                square(6)
                square(7)

                def silu(i):
                    act.wait_ge(g_done, h * TT + (RING + i + 1))
                    act.activation(pp[i % 4][:, :], pp[i % 4][:, :], ACT.Silu).then_inc(silu_done, 1)

                def turned_out(i):
                    act.wait_ge(t_done, h * TT + (i + 1))
                    act.wait_ge(stored[i % 2], h * 64 + 16 * (i // 2 + 1))
                    act.activation(turned[:, i % 2, :], pa[i % 2][:, :], ACT.Copy).then_inc(t_read, 1)

                def store(i):
                    act.wait_ge(t_read, h * TT + (RING + i + 1))
                    act.dma_start(gated_dram[h, i], turned[:, i % 2, :]).then_inc(stored[i % 2], 16)

                silu(0)
                for i in range(1, TT):
                    silu(i)
                    turned_out(i - 1)
                    store(i - 1)
                    if last and 2 <= i < 6:
                        o_split_hi(i - 2)
                turned_out(TT - 1)
                store(TT - 1)

            def later_hi(i):
                if i in (2, 3):
                    act.wait_ge(g_unit_free, 3 * HEADS + i - 1)
                elif i >= 16:
                    act.wait_ge(wo_done, 56 + 2 * (i - 15))
                else:
                    act.wait_ge(wo_done, 4 * (i - 3))
                pos = later_pos(i)
                split_hi(pos % STAGE_SLOTS, i % FLOW_SLOTS, arrived(pos))

            def o_split_hi(n):
                h, c = divmod(n, 4)
                act.wait_ge(o_in[n % 2], 16 * (n // 2 + 1))
                if c == 0 and h == 1:
                    act.wait_ge(g_done, RING + TT * HEADS)
                if c == 0 and h >= 2:
                    act.wait_ge(wo_done, 16 * (h - 1))
                act.activation(panel_part(h, 0, c), ostage[:, n % 2, :, :].rearrange("p a (d t) -> p d a t", d=4),
                               ACT.Copy).then_inc(o_hi, 1)

            with act.Fori(0, HEADS - 1) as h:
                head(h, False)
            head(HEADS - 1, True)

            later_hi(2)
            later_hi(3)
            for h in range(HEADS - 1):
                for j in range(4):
                    later_hi(4 * h + 4 + j)
                    o_split_hi(4 * h + 4 + j)

            act.wait_ge(o_taken, 16)
            for n in range(16):
                if 10 <= n < 14:
                    for k in (2 * (n - 10), 2 * (n - 10) + 1):
                        ht_write(16 + k, scaled2[k % 2], M_SH2, (scaled, KT + k + 1))
                square_half(n, (wo_read, 48 + n + 1))
                if n == 9:
                    later_hi(16)

            def hidden_hi(b, m, half, n):
                act.wait_ge(u_done, b * 8 + (n + 1))
                act.wait_ge(u_read, b * 8 + (RING + n - 1))
                act.activation(relu[n % 2], pp[n % 4][:, :], ACT.Relu).then_inc(relu_done, 1)
                act.wait_ge(relu_done, b * 8 + (n + 1))
                act.activation(ou[:, 0, m, half * HALF:(half + 1) * HALF], relu[n % 2], ACT.Square).then_inc(u_hi, 1)

            def mlp_hi(b, j, used=None):
                pos = later_pos(16 + j)
                if j < 4:
                    act.wait_ge(y_done, (b - 1) * 16 + 4 * (j + 1))
                else:
                    act.wait_ge(u_done, b * 8 + (used or 2 * (j - 3)))
                split_hi(pos % STAGE_SLOTS, j % FLOW_SLOTS, b * 32 + arrived(pos))

            later_hi(17)
            hidden_hi(0, 0, 0, 0)
            later_hi(18)
            later_hi(19)
            act.wait_ge(bc_done, 4)
            hidden_hi(0, 1, 0, 1)
            for k in range(KT):
                ht_write(24 + k, scaled2[k % 2], M_SH2, (scaled, 2 * KT + k + 1))
            for n in range(2, 8):
                half, m = divmod(n, 4)
                hidden_hi(0, m, half, n)
                if half:
                    mlp_hi(0, 4 + m, 4 + m + 1)
            for j in range(4):
                mlp_hi(1, j)
            with act.Fori(1, BLOCKS - 1) as b:
                for n in range(8):
                    m, half = divmod(n, 2)
                    hidden_hi(b, m, half, n)
                    if half:
                        mlp_hi(b, 4 + m)
                for j in range(4):
                    mlp_hi(b + 1, j)
            for n in range(8):
                m, half = divmod(n, 2)
                hidden_hi(BLOCKS - 1, m, half, n)
                if half:
                    mlp_hi(BLOCKS - 1, 4 + m)

            for n in range(16):
                square_half(16 + n, (y_read, 4 + 16 * (BLOCKS - 1) + n + 1))

        @block.vector
        def _(dve):
            vec_ = nc.vector

            def split_lo(slot, split_slot, made):
                dve.wait_ge(hi_made, made)
                vec_.tensor_tensor(wsplit[:, split_slot, 1, :], stage[:, slot, :], wsplit[:, split_slot, 0, :].bitcast(F32),
                                   ALU.subtract).then_inc(taken, 1)

            def head_lo(h, j):
                split_lo(unit_pos(0, j) % STAGE_SLOTS, j % SPLIT_SLOTS, h * HEAD_UNITS + (j + 1))

            def ada_step(k, slot, arrived, pos):
                dve.wait_ge(staged[slot], arrived)
                if k == 0:
                    vec_.tensor_scalar(ada_sum, stage[:, slot, :], cond[:, 0:1], None, ALU.mult).then_inc(taken, 1)
                else:
                    dve.wait_ge(taken, pos)
                    vec_.scalar_tensor_tensor(ada_sum, stage[:, slot, :], cond[:, k:k + 1], ada_sum,
                                              ALU.mult, ALU.add).then_inc(taken, 1)

            def mean_square(n, cols, bank, sums_count):
                dve.wait_ge(sums_done, sums_count)
                width = cols.stop - cols.start
                vec_.tensor_scalar(zcol[:, cols], bank[:, 0:width], 1.0 / D, EPS, ALU.mult, ALU.add).then_inc(z_done, 1)

            def diagonal(n, cols, out):
                dve.wait_ge(pow_done, n)
                width = cols.stop - cols.start
                vec_.tensor_tensor(out.rearrange("p (a t) -> p a t", t=P),
                                   ident[:, :].unsqueeze(1).to_broadcast([P, width, P]),
                                   rcol[:, cols].unsqueeze(2).to_broadcast([P, width, P]), ALU.mult).then_inc(diag_done, 1)

            def half_cols(half):
                return slice(4 * half, 4 * half + 4)

            def ht_lo(n, source, shift):
                half, k = divmod(n % 16, KT)
                part = slice(half * HALF, (half + 1) * HALF)
                dve.wait_ge(ht_hi, n + 1)
                vec_.scalar_tensor_tensor(ht[:, 1, k, part], source, mods[:, shift + k:shift + k + 1],
                                          ht[:, 0, k, part].bitcast(F32), ALU.add, ALU.subtract).then_inc(ht_done, 1)

            dve.wait_ge(cond_done, 1)
            for k in range(KT):
                ada_step(k, k % STAGE_SLOTS, 16 * (k // STAGE_SLOTS + 1), k)
            for k in range(KT):
                dve.wait_ge(squared, k + 1)
                if k == 0:
                    vec_.tensor_copy(sums1, squares1[0]).then_inc(sq_added, 1)
                else:
                    dve.wait_ge(sq_added, k)
                    vec_.tensor_tensor(sums1, sums1, squares1[k % 2], ALU.add).then_inc(sq_added, 1)
            dve.wait_ge(ada_done, 1)
            vec_.tensor_tensor(mods[:, M_SC1:M_SC1 + KT], pp[0][:, 0:8],
                               vecs[:, C_ADAB + M_SC1:C_ADAB + M_SC1 + KT], ALU.add).then_inc(mods_done, 1)
            dve.wait_ge(mods_done, 1)
            vec_.scalar_tensor_tensor(gains[:, 0, :], mods[:, M_SC1:M_SC1 + KT], 1.0, vecs[:, C_GMIX:C_GMIX + KT],
                                      ALU.add, ALU.mult).then_inc(gains_done, 1)

            def sh1_step(k):
                pos = KT + 1 + k
                ada_step(k, pos % STAGE_SLOTS, 16 * (pos // STAGE_SLOTS + 1), pos)

            def prescale(n):
                half, k = divmod(n, KT)
                x_part = qkv[:, k, half * HALF:(half + 1) * HALF]
                if k == 0:
                    dve.wait_ge(bc_done, half + 1)
                vec_.scalar_tensor_tensor(x_part, x_part, gains[:, 0, k:k + 1], pa[half][:, :], ALU.mult, ALU.mult)\
                    .then_inc(scaled, 1)

            mean_square(1, slice(0, KT), pa[2], 1)
            split_lo(0, 0, 1)
            sh1_step(0)
            diagonal(1, slice(0, KT), diag1)
            sh1_step(1)
            sh1_step(2)
            for k in range(3, KT):
                sh1_step(k)
                if k >= 4:
                    prescale(2 * k - 8)
                    prescale(2 * k - 7)
            dve.wait_ge(ada_done, 2)
            vec_.tensor_tensor(mods[:, M_SH1:M_SH1 + KT], pp[1][:, 0:8],
                               vecs[:, C_ADAB + M_SH1:C_ADAB + M_SH1 + KT], ALU.add).then_inc(mods_done, 1)
            dve.wait_ge(mods_done, 2)
            for n in range(16):
                half, k = divmod(n, KT)
                ht_lo(n, qkv[:, k, half * HALF:(half + 1) * HALF], M_SH1)
                if n == KT:
                    split_lo(1, 1, 2)

            dve.wait_ge(trig_in, 16)
            def head(h, last):
                for j in range(2, 6):
                    head_lo(h, j)
                for n in range(8):
                    m, half = divmod(n, 2)
                    part = slice(half * HALF, (half + 1) * HALF)
                    cos, sin = trig[:, 0, part], trig[:, 1, part]
                    psum = pp[n % 4][:, :]
                    dve.wait_ge(qk_done, h * 8 + (n + 1))
                    if m % 2 == 0:
                        vec_.tensor_tensor(qkv[:, m, part], psum, cos, ALU.mult)
                        vec_.tensor_tensor(qkv[:, m + 1, part], psum, sin, ALU.mult).then_inc(qk_read, 1)
                    else:
                        t1, t2 = rope_tmp[2 * half], rope_tmp[2 * half + 1]
                        vec_.tensor_tensor(t1, psum, sin, ALU.mult)
                        vec_.tensor_tensor(t2, psum, cos, ALU.mult).then_inc(qk_read, 1)
                        dve.wait_ge(qk_read, h * 8 + (n + 1))
                        vec_.tensor_tensor(qkv[:, m - 1, part], qkv[:, m - 1, part], t1, ALU.subtract)
                        vec_.tensor_tensor(qkv[:, m, part], qkv[:, m, part], t2, ALU.add).then_inc(roped, 1)
                    if half == 1:
                        head_lo(h, 6 + m)

                for k in range(KT):
                    pos = head_pos(0, KT + k)
                    ada_step(k, pos % STAGE_SLOTS, h * (16 * HEAD_STREAM // STAGE_SLOTS) + 16 * (pos // STAGE_SLOTS + 1),
                             head_pos(h, KT + k))
                dve.wait_ge(ada_done, h + 3)
                vec_.tensor_tensor(mods[:, bass.ds(h * 8 + 16, 8)], pa[2][:, 0:8],
                                   vecs[:, bass.ds(h * 8 + (C_ADAB + 16), 8)], ALU.add).then_inc(mods_done, 1)

                def scores(c):
                    dve.wait_ge(sc_done, h * NCHUNK + (c + 1))
                    vec_.tensor_tensor(sc[:, c % 2, :], pa[c % 2][:, 0:384], hc[:, H_MASK:H_MASK + 384], ALU.mult)\
                        .then_inc(sc_read, 1)

                def new_state(c):
                    dve.wait_ge(kv_done, h * 3 + (c + 1))
                    if c:
                        dve.wait_ge(state_done, h * 3 + c)
                    for a in range(2):
                        if c == 0:
                            last = vec_.tensor_copy(state[:, 0, a, :], pp[a][:, :])
                        else:
                            last = vec_.scalar_tensor_tensor(state[:, c % 2, a, :], state[:, (c - 1) % 2, a, :],
                                                             hc[:, H_DECAY:H_DECAY + 1], pp[a][:, :], ALU.mult, ALU.add)
                    last.then_inc(state_done, 1)

                def normalise(i):
                    dve.wait_ge(row_scale, h * TT + (i + 2))
                    vec_.tensor_scalar(og[:, i, :], pa[2 + i % 2][:, :], rs[:, 2, i % 2:i % 2 + 1], math.sqrt(DV),
                                       ALU.mult, ALU.mult)\
                        .then_inc(o_read, 1)

                dve.wait_ge(hc_in, h * 16 + 16)
                scores(0)
                scores(1)
                new_state(0)
                head_lo(h, 10)
                normalise(0)
                normalise(1)
                new_state(1)
                scores(2)
                head_lo(h, 11)
                normalise(2)
                normalise(3)
                new_state(2)
                scores(3)
                head_lo(h, 12)
                normalise(4)
                normalise(5)
                head_lo(h, 13)
                normalise(6)
                normalise(7)
                dve.wait_ge(o_read, h * TT + (2 + TT))
                for i in range(TT):
                    dve.wait_ge(silu_done, h * TT + (i + 1))
                    vec_.tensor_tensor(og[:, i, :], og[:, i, :], pp[i % 4][:, :], ALU.mult).then_inc(gated, 1)
                    if last and 2 <= i < 6:
                        o_split_lo(i - 2)

            def o_split_lo(n):
                h, c = divmod(n, 4)
                dve.wait_ge(o_hi, n + 1)
                vec_.tensor_tensor(panel_part(h, 1, c), ostage[:, n % 2, :, :].rearrange("p a (d t) -> p d a t", d=4),
                                   panel_part(h, 0, c).bitcast(F32), ALU.subtract).then_inc(o_taken, 1)

            with dve.Fori(0, HEADS - 1) as h:
                head(h, False)
            head(HEADS - 1, True)

            dve.wait_ge(mods_done, 6)
            vec_.tensor_scalar(gains[:, 1, :], mods[:, M_GT1:M_GT1 + KT], 1.0, None, ALU.add)
            vec_.tensor_scalar(gains[:, 2, :], mods[:, M_GT2:M_GT2 + KT], 1.0, None, ALU.add)
            vec_.scalar_tensor_tensor(gains[:, 3, :], mods[:, M_SC2:M_SC2 + KT], 1.0, vecs[:, C_GMLP:C_GMLP + KT],
                                      ALU.add, ALU.mult).then_inc(gains_done, 1)
            dve.wait_ge(gains_done, 2)

            def later_lo(i):
                split_lo(later_pos(i) % STAGE_SLOTS, i % FLOW_SLOTS, W_OUT0 + i + 1)

            def residual(m, half, psum, gate, read):
                part = slice(half * HALF, (half + 1) * HALF)
                vec_.scalar_tensor_tensor(x1[:, m, part], psum[:, :], gains[:, gate, m:m + 1], x1[:, m, part],
                                          ALU.mult, ALU.add).then_inc(read, 1)

            later_lo(2)
            later_lo(3)
            for h in range(HEADS - 1):
                for j in range(4):
                    for g in range(4 * j, 4 * j + 4):
                        m, half = divmod(g, 2)
                        if h == 0:
                            dve.wait_ge(x_in[m], 32)
                        dve.wait_ge(wo_done, 16 * h + g + 1)
                        residual(m, half, pp[g % 4], 1, wo_read)
                    later_lo(4 * h + 4 + j)
                    o_split_lo(4 * h + 4 + j)

            def scale(n):
                half, k = divmod(n, KT)
                if k == 0:
                    dve.wait_ge(bc_done, 2 + half + 1)
                if n >= 2:
                    dve.wait_ge(ht_done, 16 + n - 1)
                vec_.scalar_tensor_tensor(scaled2[n % 2], x1[:, k, half * HALF:(half + 1) * HALF],
                                          gains[:, 3, k:k + 1], pa[half][:, :], ALU.mult, ALU.mult).then_inc(scaled, 1)

            for n in range(16):
                half, m = divmod(n, KT)
                if n == 9:
                    mean_square(2, half_cols(0), pa[2], 2)
                    diagonal(2, half_cols(0), sums[0])
                if 10 <= n < 14:
                    for k in (2 * (n - 10), 2 * (n - 10) + 1):
                        scale(k)
                        if k:
                            ht_lo(16 + k - 1, scaled2[(k - 1) % 2], M_SH2)
                if n == 14:
                    ht_lo(16 + 7, scaled2[1], M_SH2)
                dve.wait_ge(wo_done, 48 + n + 1)
                residual(m, half, pp[n % 4], 1, wo_read)
                if n == 9:
                    later_lo(16)

            def hidden_lo(b, m, half, n):
                psum = pp[n % 4][:, :]
                part = slice(half * HALF, (half + 1) * HALF)
                dve.wait_ge(relu_done, b * 8 + (n + 1))
                vec_.scalar_tensor_tensor(psum, psum, 0.0, relu[n % 2], ALU.max, ALU.mult).then_inc(u_sq, 1)
                dve.wait_ge(u_hi, b * 8 + (n + 1))
                dve.wait_ge(u_sq, b * 8 + (n + 1))
                vec_.tensor_tensor(ou[:, 1, m, part], psum, ou[:, 0, m, part].bitcast(F32), ALU.subtract).then_inc(u_read, 1)

            def mlp_lo(b, j):
                split_lo(later_pos(16 + j) % STAGE_SLOTS, j % FLOW_SLOTS, b * 8 + (W_MLP0 + j + 1))

            def outputs(b):
                for g in range(16):
                    m, half = divmod(g, 2)
                    dve.wait_ge(y_done, b * 16 + (g + 1))
                    residual(m, half, pa[g % 4], 2, y_read)
                    if g % 4 == 3:
                        mlp_lo(b + 1, g // 4)

            later_lo(17)
            mean_square(3, half_cols(1), pa[3], 3)
            hidden_lo(0, 0, 0, 0)
            later_lo(18)
            later_lo(19)
            diagonal(3, half_cols(1), sums[1])
            hidden_lo(0, 1, 0, 1)
            for n in range(KT, 16):
                scale(n)
                if n > KT:
                    ht_lo(16 + n - 1, scaled2[(n - 1) % 2], M_SH2)
            ht_lo(31, scaled2[1], M_SH2)
            for n in range(2, 8):
                half, m = divmod(n, 4)
                hidden_lo(0, m, half, n)
                if half:
                    mlp_lo(0, 4 + m)
            outputs(0)
            with dve.Fori(1, BLOCKS - 1) as b:
                for n in range(8):
                    m, half = divmod(n, 2)
                    hidden_lo(b, m, half, n)
                    if half:
                        mlp_lo(b, 4 + m)
                outputs(b)
            for n in range(8):
                m, half = divmod(n, 2)
                hidden_lo(BLOCKS - 1, m, half, n)
                if half:
                    mlp_lo(BLOCKS - 1, 4 + m)

            def final(n):
                half, k = divmod(n, KT)
                slot, use = out_slot(n)
                if k == 0:
                    dve.wait_ge(bc_done, 4 + half + 1)
                if use:
                    dve.wait_ge(out_stored[slot], 16 * use)
                vec_.scalar_tensor_tensor(outs[slot], x1[:, k, half * HALF:(half + 1) * HALF],
                                          vecs[:, C_GFIN + k:C_GFIN + k + 1], pp[half][:, :], ALU.mult, ALU.mult)\
                    .then_inc(out_ready, 1)

            for n in range(16):
                half, m = divmod(n, KT)
                if n == 9:
                    mean_square(4, half_cols(0), pp[2], 4)
                    diagonal(4, half_cols(0), sums[0])
                if 10 <= n < 14:
                    final(2 * (n - 10))
                    final(2 * (n - 10) + 1)
                dve.wait_ge(y_done, 16 * (BLOCKS - 1) + n + 1)
                residual(m, half, pa[n % 4], 2, y_read)
            mean_square(5, half_cols(1), pp[3], 5)
            diagonal(5, half_cols(1), sums[1])
            for n in range(KT, 16):
                final(n)

        @block.tensor
        def _(pe):
            mm = nc.tensor.matmul

            def product(out, stationary, moving, start, stop):
                mm(out, stationary(0), moving(0), start=start, stop=False)
                mm(out, stationary(0), moving(1), start=False, stop=False)
                return mm(out, stationary(1), moving(0), start=False, stop=stop)

            def by_feature(slot, tile):
                return lambda part: wsplit[:, slot, part, tile * P:(tile + 1) * P]

            def half_of(x, k, half):
                return lambda part: x[:, part, k, half * HALF:(half + 1) * HALF]

            def token_sums(sq, columns, bank, first, last):
                for j in range(columns):
                    done = mm(bank[:, j:j + 1], sq[:, j * P:(j + 1) * P], ones[:, 0:1],
                              start=first and j == 0, stop=last, skip_group_check=True)
                done.then_inc(sums_done, 1)

            def broadcast(bank, diag):
                mm(bank[:, :], ones[:, :], diag, start=True, stop=True).then_inc(bc_done, 1)

            def ada_total(bank, column, acc):
                for m in range(KT):
                    last = mm(bank[:, column + m:column + m + 1], acc[:, m * P:(m + 1) * P], ones[:, 0:1],
                              start=True, stop=True)
                last.then_inc(ada_done, 1)

            pe.sem_inc(g_unit_free, 3)
            pe.sem_inc(g_done, RING)
            pe.sem_inc(gated, RING)
            pe.sem_inc(o_squared, RING)
            pe.sem_inc(o_read, 2)
            pe.sem_inc(t_read, RING)
            pe.sem_inc(row_scale, 1)
            pe.sem_inc(stored[0], 16)
            pe.sem_inc(stored[1], 16)
            pe.sem_inc(u_read, RING)
            pe.sem_inc(y_read, 4)

            pe.wait_ge(setup_done, 2)
            def keep_warm(n):
                for _ in range(n):
                    mm(pa[3][:, 0:P], ones[:, :], ones[:, :], start=True, stop=True)

            pe.wait_ge(taken, KT)
            ada_total(pp[0], 0, ada_sum)
            keep_warm(30)
            pe.wait_ge(sq_added, KT)
            token_sums(sums1, TT, pa[2], True, True)
            keep_warm(8)
            pe.wait_ge(diag_done, 1)
            for half in range(2):
                broadcast(pa[half], diag1[:, half * HALF:(half + 1) * HALF])
            keep_warm(30)
            pe.wait_ge(taken, 2 * KT + 1)
            ada_total(pp[1], 0, ada_sum)

            def head(h):
                for m in range(4):
                    pe.wait_ge(taken, unit_pos(h, m) + 1)
                    for half in range(2):
                        n = 2 * m + half
                        if n < 4:
                            pe.wait_ge(gated, h * TT + (5 + n))
                        else:
                            pe.wait_ge(qk_read, h * TT + (n - 3))
                        for k in range(KT):
                            if m == 0:
                                pe.wait_ge(ht_done, 8 * half + k + 1)
                            last = product(pp[n % 4][:, :], by_feature(m, k), half_of(ht, k, half), k == 0, k == KT - 1)
                        last.then_inc(qk_done, 1)

                def token_panel(i, first_unit, free):
                    for k in range(KT):
                        u, slot = divmod(k, 2)[0], (first_unit + k // 2) % SPLIT_SLOTS
                        last = product(pp[i % 4][:, :], lambda part: ht[:, part, k, i * P:(i + 1) * P],
                                       lambda part: wsplit[:, slot, part, (k % 2) * DV:(k % 2 + 1) * DV], k == 0, k == KT - 1)
                        if i == TT - 1 and k in (1, 3, 5):
                            last.then_inc(free, 1)
                    return last

                for i in range(TT):
                    if i == 0:
                        pe.wait_ge(taken, unit_pos(h, 7) + 1)
                    if i < 4:
                        pe.wait_ge(qk_read, h * TT + (5 + i))
                    else:
                        pe.wait_ge(v_read, h * TT + (i - 3))
                    token_panel(i, 4, v_unit_free).then_inc(v_done, 1)

                pe.wait_ge(o_read, h * TT + 2)
                pe.wait_ge(taken, head_pos(h, KT + KT - 1) + 1)
                ada_total(pa[2], 0, ada_sum)

                def scores(c):
                    if c < 2:
                        pe.wait_ge(t_read, h * TT + RING)
                    else:
                        pe.wait_ge(sc_read, h * NCHUNK + (c - 1))
                    t0 = c * CHUNK
                    for a in range(2):
                        mm(pa[c % 2][:, 0:256], qkv[:, 2 + a, t0:t0 + P], qkv[:, a, t0:t0 + 256], start=a == 0, stop=a == 1)
                    for a in range(2):
                        last = mm(pa[c % 2][:, 256:384], qkv[:, 2 + a, t0 + P:t0 + 256], qkv[:, a, t0 + P:t0 + 256],
                                  start=a == 0, stop=a == 1)
                    last.then_inc(sc_done, 1)

                def keys(c):
                    if c < 2:
                        pe.wait_ge(v_read, h * TT + (7 + c))
                    else:
                        pe.wait_ge(kt_read, h * 3 + 1)
                    for s in range(2):
                        for a in range(2):
                            col = s * DK + a * P
                            t0 = c * CHUNK + s * P
                            last = nc.tensor.transpose(pp[2 + c % 2][:, col:col + P], qkv[:, 2 + a, t0:t0 + P], ident[:, :])
                    last.then_inc(kt_done, 1)

                def keys_values(c):
                    if c == 0:
                        pe.wait_ge(v_read, h * TT + TT)
                    else:
                        pe.wait_ge(state_done, h * 3 + c)
                    pe.wait_ge(kt_read, h * 3 + (c + 1))
                    for a in range(2):
                        for s in range(2):
                            last = mm(pp[a][:, :], kn[:, c % 2, s, a * P:(a + 1) * P], v[:, 2 * c + s, :],
                                      start=s == 0, stop=s == 1)
                    last.then_inc(kv_done, 1)

                def outputs(i):
                    c, par = divmod(i, 2)
                    pe.wait_ge(o_read, h * TT + (i + 1))
                    if i == 0:
                        pe.wait_ge(mods_done, h + 3)
                    pe.wait_ge(sc_read, h * NCHUNK + (c + 1))
                    bank = pa[2 + par][:, :]
                    pairs = [(sc[:, c % 2, (s + par) * P:(s + par + 1) * P], v[:, 2 * c + s, :]) for s in range(par + 1)]
                    if c:
                        pe.wait_ge(state_done, h * 3 + c)
                        pairs += [(qkv[:, a, i * P:(i + 1) * P], state[:, (c - 1) % 2, a, :]) for a in range(2)]
                    for n, (stationary, moving) in enumerate(pairs):
                        last = mm(bank, stationary, moving, start=n == 0, stop=n == len(pairs) - 1)
                    last.then_inc(o_done, 1)

                pe.wait_ge(roped, h * 4 + 4)
                scores(0)
                keys(0)
                scores(1)
                keys(1)
                keys_values(0)
                outputs(0)
                outputs(1)
                keys_values(1)
                scores(2)
                keys(2)
                outputs(2)
                outputs(3)
                keys_values(2)
                scores(3)
                for i in range(4, 8):
                    outputs(i)

                def turn(i):
                    if i < 2:
                        pe.wait_ge(sc_read, h * NCHUNK + (3 + i))
                    else:
                        pe.wait_ge(t_read, h * TT + (RING + i - 1))
                    pe.wait_ge(gated, h * TT + (RING + i + 1))
                    for d in range(4):
                        last = nc.tensor.transpose(pa[i % 2][:, d * P:(d + 1) * P], og[:, i, d * P:(d + 1) * P], ident[:, :])
                    last.then_inc(t_done, 1)

                pe.wait_ge(taken, unit_pos(h, 11) + 1)
                pe.wait_ge(state_done, h * 3 + 3)
                pe.wait_ge(kt_read, h * 3 + 3)
                for i in range(TT):
                    if i >= 4:
                        pe.wait_ge(gated, h * TT + (RING + i - 3))
                    token_panel(i, 8, g_unit_free).then_inc(g_done, 1)
                    if i:
                        turn(i - 1)
                turn(TT - 1)

            with pe.Fori(0, HEADS) as h:
                head(h)

            for h in range(HEADS):
                for g in range(16):
                    m, half = divmod(g, 2) if h < 3 else divmod(g, KT)[::-1]
                    if h == 0 and g < 4:
                        pe.wait_ge(gated, TT * HEADS + 5 + g)
                    else:
                        pe.wait_ge(wo_read, 16 * h + g - 3)
                    if m == 0:
                        pe.wait_ge(o_taken, 4 * h + 2 * (half + 1))
                    if m % 2 == 0 and half == 0:
                        pe.wait_ge(taken, later_pos(4 * h + m // 2) + 1)
                    for k in range(4):
                        last = product(pp[g % 4][:, :], by_feature(m // 2, (m % 2) * 4 + k), panel_half(h, k, half),
                                       k == 0, k == 3)
                    last.then_inc(wo_done, 1)
                    if h == 3 and g == 8:
                        pe.wait_ge(sq_added, 2 * KT)
                        token_sums(sums[0], 4, pa[2], True, True)
                    if h == 3 and g == 9:
                        pe.wait_ge(diag_done, 2)
                        broadcast(pa[0], sums[0])

            pe.wait_ge(wo_read, 64)

            def hidden(b, m, half, n, new_unit):
                if new_unit:
                    pe.wait_ge(taken, b * 8 + (later_pos(16 + m) + 1))
                pe.wait_ge(u_read, b * 8 + (RING + n - 3))
                for k in range(KT):
                    if m == 0:
                        pe.wait_ge(ht_done, 16 + 8 * half + k + 1)
                    last = product(pp[n % 4][:, :], by_feature(m, k), half_of(ht, k, half), k == 0, k == KT - 1)
                last.then_inc(u_done, 1)

            def second(b, m, half, n, ks, wait):
                for k in ks:
                    if wait:
                        pe.wait_ge(u_read, b * 8 + (RING + 2 * k + half + 1))
                    last = product(pa[n % 4][:, :], by_feature(m // 2, (m % 2) * 4 + k), half_of(ou, k, half), k == 0, k == 3)
                return last

            def outputs(b, order, after=None):
                for n, (m, half) in enumerate(order):
                    if (m % 2, half) == (0, 0):
                        pe.wait_ge(taken, b * 8 + (later_pos(16 + 4 + m // 2) + 1))
                    pe.wait_ge(y_read, b * 16 + (n + 1))
                    if n < 4:
                        second(b, m, half, n, range(3), True)
                        if n == 3:
                            for n2, (m2, half2) in enumerate(order[:4]):
                                second(b, m2, half2, n2, [3], True).then_inc(y_done, 1)
                    else:
                        second(b, m, half, n, range(4), n == KT).then_inc(y_done, 1)
                    if after:
                        after(n)

            by_tile = [(m, half) for m in range(KT) for half in range(2)]
            by_half = [(m, half) for half in range(2) for m in range(KT)]

            for n in range(8):
                half, m = divmod(n, 4)
                hidden(0, m, half, n, half == 0)
                if n == 0:
                    pe.wait_ge(sq_added, KT + 16)
                    token_sums(sums[1], 4, pa[3], True, True)
                if n == 1:
                    pe.wait_ge(diag_done, 3)
                    broadcast(pa[1], sums[1])
            pe.wait_ge(u_read, RING + 7)
            outputs(0, by_tile)
            with pe.Fori(1, BLOCKS - 1) as b:
                for n in range(8):
                    m, half = divmod(n, 2)
                    hidden(b, m, half, n, half == 0)
                outputs(b, by_tile)
            for n in range(8):
                m, half = divmod(n, 2)
                hidden(BLOCKS - 1, m, half, n, half == 0)

            def final_norm(n):
                if n == 8:
                    pe.wait_ge(sq_added, KT + 16 + KT)
                    token_sums(sums[0], 4, pp[2], True, True)
                if n == 9:
                    pe.wait_ge(diag_done, 4)
                    broadcast(pp[0], sums[0])
            outputs(BLOCKS - 1, by_half, final_norm)
            pe.wait_ge(sq_added, KT + 32)
            token_sums(sums[1], 4, pp[3], True, True)
            pe.wait_ge(diag_done, 5)
            broadcast(pp[1], sums[1])



def kernel(**inputs):
    import numpy as _np
    import concourse.bacc as _bacc
    from concourse import mybir as _mybir
    from concourse.bass_utils import run_bass_kernel_spmd as _run

    f = {k: _np.asarray(a) for k, a in inputs.items()}

    def columns(a):
        return a.reshape(-1, P).T

    def rows(a):
        return a.reshape(-1, P, a.shape[-1])

    w_in = f["ret_w_in"][0]
    q, k, val, gate = (w_in[:, a:b] for a, b in ((0, D), (D, 2 * D), (2 * D, 4 * D), (4 * D, 6 * D)))
    units = []
    for h in range(HEADS):
        for m in (q, k):
            part = rows(m)[:, :, h * DK:(h + 1) * DK]
            for odd in range(2):
                units.append(part[:, :, odd::2].transpose(1, 0, 2).reshape(P, UNIT))
        for m in (val, gate):
            part = rows(m)[:, :, h * DV:(h + 1) * DV]
            for j in range(4):
                units.append(part[2 * j:2 * j + 2].transpose(1, 0, 2).reshape(P, UNIT))

    def panel(w):
        r = w.reshape(4, P, 4, 2, P).transpose(2, 1, 3, 0, 4)
        return [r[j].reshape(P, UNIT) for j in range(4)]

    for h in range(HEADS):
        units += panel(f["ret_w_out"][0][h * DV:(h + 1) * DV])
    for b in range(BLOCKS):
        w1 = rows(f["mlp_w1"][0])[:, :, b * HALF:(b + 1) * HALF]
        units += [w1[:, :, m * P:(m + 1) * P].transpose(1, 0, 2).reshape(P, UNIT) for m in range(4)]
        units += panel(f["mlp_w2"][0][b * HALF:(b + 1) * HALF])

    vec = _np.concatenate([columns(a) for a in (f["c"][0], f["ada_b"][0], f["norm_mix_g"][0], f["norm_mlp_g"][0],
                                                f["final_norm_g"])], axis=1)
    rope, heads, eye = constants()
    arrays = {
        "xT": f["x"][0].T.reshape(KT, P, T),
        "vec": vec,
        "ada": f["ada_w"][0].reshape(KT, P, 6, D).transpose(2, 0, 1, 3),
        "weights": _np.stack(units),
        "rope": rope, "heads": heads, "eye": eye,
    }
    arrays = {name: _np.ascontiguousarray(a) for name, a in arrays.items()}
    nc = _bacc.Bacc("TRN2", target_bir_lowering=False, num_devices=1)
    args = [nc.dram_tensor(name, a.shape, _mybir.dt.from_np(a.dtype), kind="ExternalInput").ap() for name, a in arrays.items()]
    out = nc.dram_tensor("outT", (KT, P, T), _mybir.dt.float32, kind="ExternalOutput").ap()
    build(nc, *args, out)
    r = _run(nc, [arrays], core_ids=[0])
    return r.results[0]["outT"].reshape(D, T).T.reshape(1, T, D)
```

```python
import math
from contextlib import ExitStack

import numpy as np
import concourse.bass as bass
from concourse import mybir

F32 = mybir.dt.float32
F32R = mybir.dt.float32r
ALU = mybir.AluOpType
ACT = mybir.ActivationFunctionType

P = 128
D = 1024
T = 1024
KT = D // P
HALF = 512
HEADS = 4
DK = D // HEADS
DV = 2 * D // HEADS
FF = 4 * D
CHUNK = 256
NCHUNK = T // CHUNK
TT = T // P
UNIT = 1024
STAGE_SLOTS = 4
SPLIT_SLOTS = 6
FLOW_SLOTS = 4
BLOCKS = FF // HALF
EPS = 1e-6

C_COND, C_ADAB, C_GMIX, C_GMLP, C_GFIN, N_VEC = 0, 8, 56, 64, 72, 80
H_MASK, H_EPS, H_ZETA, H_DECAY, N_HEAD = 0, 384, 386, 388, 390
M_SH1, M_SC1, M_GT1, M_SH2, M_SC2, M_GT2 = range(0, 48, 8)

ADA_FIRST = 2 * KT
SH1_SPLIT = 7
HEAD_UNITS = 12
HEAD_STREAM = HEAD_UNITS + KT
START = [("a", 1, k) for k in range(KT)] + [("w", 0, 0)] + [("a", 0, k) for k in range(KT)] + [("w", 1, 0)]
STREAM = [("w", j) for j in range(2, 10)] + [("a", k) for k in range(KT)] + [("w", j) for j in range(10, 14)]
W_OUT0 = HEADS * HEAD_UNITS
W_MLP0 = W_OUT0 + 4 * HEADS


def constants():
    inv = np.float32(10000.0) ** (-np.linspace(0.0, 1.0, DK // 2, dtype=np.float32))
    ang = (np.arange(T, dtype=np.float32)[:, None] * inv[None, :].astype(np.float32)).astype(np.float32)
    rope = np.stack([np.cos(ang).T, np.sin(ang).T], axis=1).astype(np.float32)
    lg = np.log1p(-np.exp2(-5.0 - np.arange(HEADS)))
    s = np.arange(P)[:, None]
    t = np.arange(P)[None, :]
    tri = (s <= t).astype(np.float64)
    k_scale = DK ** -0.5
    heads = np.zeros((HEADS, P, N_HEAD))
    for h in range(HEADS):
        down = np.exp(-(s + 1.0) * lg[h]) * k_scale
        heads[h, :, 0:128] = tri * down
        heads[h, :, 128:256] = down
        heads[h, :, 256:384] = tri * np.exp(-(s + 129.0) * lg[h]) * k_scale
        for a in range(2):
            xi = np.exp((s[:, 0] + 128 * a + 1.0) * lg[h])
            heads[h, :, H_EPS + a] = DV * EPS / (xi * xi)
            heads[h, :, H_ZETA + a] = np.exp((CHUNK - 1.0 - 128 * a - s[:, 0]) * lg[h]) * k_scale
        heads[h, :, H_DECAY] = np.exp(CHUNK * lg[h])
    return rope, heads.astype(np.float32), np.eye(P, dtype=np.float32)


def build(nc, xT, vec, ada, weights, rope, heads, eye, outT):
    ctx = ExitStack()
    with ctx:
        def sem(name):
            return ctx.enter_context(nc.semaphore(name))

        def sb(name, shape, dt=F32, into=ctx):
            return into.enter_context(nc.sbuf_tensor(name, shape, dt))

        ht = sb("ht", [P, 2, KT, T], F32R)
        stage = sb("stage", [P, STAGE_SLOTS, UNIT])
        wsplit = sb("wsplit", [P, SPLIT_SLOTS, 2, UNIT], F32R)
        vecs = sb("vecs", [P, N_VEC])
        mods = sb("mods", [P, 48])
        gains = sb("gains", [P, 4, KT])
        cond = sb("cond", [P, KT])
        ident = sb("ident", [P, P])
        ones = sb("ones", [P, P])
        power = sb("power", [P, KT])
        zcol = sb("zcol", [P, KT])
        rcol = sb("rcol", [P, KT])

        before_v = ExitStack()
        xin = sb("xin", [P, KT, T], into=before_v)
        before_v.close()
        before_v = ExitStack()
        sb("v_hi_bytes", [P, TT, DV], into=before_v)
        rope_tmp = sb("rope_tmp", [P, 4, HALF], into=before_v)
        before_v.close()
        first = ExitStack()
        vs = sb("vs", [P, 2, TT, DV], F32R, into=first)
        qk = sb("qk", [P, 4, T], into=first)
        turned = sb("turned", [P, 2, DV], into=first)
        hc = sb("hc", [P, N_HEAD], into=first)
        rs = sb("rs", [P, 3, 2], into=first)
        before_chunks = ExitStack()
        trig = sb("trig", [P, 2, T], into=before_chunks)
        before_chunks.close()
        scs = sb("scs", [P, 2, 384], F32R, into=first)
        kn = sb("kn", [P, 2, 2, DK], F32R, into=first)
        qs = sb("qs", [P, 2, 2, CHUNK], F32R, into=first)
        state = sb("state", [P, 2 * DV], into=first)
        sts = sb("sts", [P, 2, 2 * DV], F32R, into=first)
        first.close()
        qk_row = qk[:, :, :].rearrange("p a n -> p (a n)")
        ada_sum = turned[:, :, :].rearrange("p a n -> p (a n)")
        sums1 = qk_row[:, 0:UNIT]
        squares1 = [qk_row[:, (1 + i) * UNIT:(2 + i) * UNIT] for i in range(2)]
        diag1 = qk_row[:, 3 * UNIT:4 * UNIT]
        rms_half = squares1[0][:, 0:HALF]

        later = ExitStack()
        ou = sb("ou", [P, 2, 4, T], F32R, into=later)
        x1 = sb("x1", [P, KT, T], into=later)
        ostage = sb("ostage", [P, 2, 2, DV], into=later)
        spare = sb("spare", [P, 2, HALF], into=later)
        later.close()
        rows4 = ostage[:, :, :, :].rearrange("p a b n -> p (a b) n")
        squares2 = [rows4[:, i] for i in range(2)]
        scaled2 = [rows4[:, 2 + i] for i in range(2)]
        relu = [spare[:, i] for i in range(2)]
        sums = [spare[:, i] for i in range(2)]

        pp = [ctx.enter_context(nc.psum_tensor(f"pp{i}", [P, HALF], F32)) for i in range(4)]
        pa = [ctx.enter_context(nc.psum_tensor(f"pa{i}", [P, HALF], F32)) for i in range(4)]

        gated_dram = nc.dram_tensor("gated_T", (HEADS, TT, P, DV), F32, kind="Internal").ap()

        consts_in, trig_in = sem("consts_in"), sem("trig_in")
        x_in = [sem(f"x_in{k}") for k in range(KT)]
        staged = [sem(f"staged{i}") for i in range(STAGE_SLOTS)]
        taken = sem("taken")
        hi_made = sem("hi_made")
        setup_done = sem("setup_done")
        cond_done = sem("cond_done")
        ada_done = sem("ada_done")
        mods_done = sem("mods_done")
        gains_done = sem("gains_done")
        squared = sem("squared")
        sq_added = sem("sq_added")
        sums_done = sem("sums_done")
        z_done, pow_done, diag_done, bc_done = sem("z_done"), sem("pow_done"), sem("diag_done"), sem("bc_done")
        scaled, ht_hi, ht_done = sem("scaled"), sem("ht_hi"), sem("ht_done")
        gained = sem("gained")
        rms_copied = sem("rms_copied")
        scaled_2 = sem("scaled_2")
        qk_done, qk_read, roped = sem("qk_done"), sem("qk_read"), sem("roped")
        v_hi = sem("v_hi")
        v_done, v_read, v_unit_free = sem("v_done"), sem("v_read"), sem("v_unit_free")
        sc_done, sc_masked, sc_hi, sc_read = sem("sc_done"), sem("sc_masked"), sem("sc_hi"), sem("sc_read")
        kt_done, kn_hi, kt_read = sem("kt_done"), sem("kn_hi"), sem("kt_read")
        q_hi, q_split = sem("q_hi"), sem("q_split")
        kv_done, state_new, state_hi, state_done = sem("kv_done"), sem("state_new"), sem("state_hi"), sem("state_done")
        o_done, o_squared, row_scale, o_read = sem("o_done"), sem("o_squared"), sem("row_scale"), sem("o_read")
        scale_step = sem("scale_step")
        g_done, silu_done, gated, g_unit_free = sem("g_done"), sem("silu_done"), sem("gated"), sem("g_unit_free")
        t_done, t_read = sem("t_done"), sem("t_read")
        hc_in = sem("hc_in")
        stored = [sem("stored0"), sem("stored1")]
        o_in = [sem("o_in0"), sem("o_in1")]
        o_hi, o_taken = sem("o_hi"), sem("o_taken")
        wo_done, wo_read = sem("wo_done"), sem("wo_read")
        u_done, relu_done, u_sq, u_hi, u_read = sem("u_done"), sem("relu_done"), sem("u_sq"), sem("u_hi"), sem("u_read")
        y_done, y_read = sem("y_done"), sem("y_read")
        out_ready = sem("out_ready")
        out_stored = sem("out_stored")

        RING = 8

        block = ctx.enter_context(nc.Block())

        def head_pos(h, idx):
            return h * HEAD_STREAM + ADA_FIRST + 2 + idx

        def unit_pos(h, j):
            return h * HEAD_STREAM + ADA_FIRST + j + (KT if j in (10, 11, 12, 13) else 0)

        def output_tile(i):
            return qk[:, :, i * P:(i + 1) * P]

        keys_bank = [pa[3], pp[2], pp[3]]

        def by_output(bank):
            return bank[:, :].rearrange("p (d t) -> p d t", d=4)

        def panel_half(h, k, half):
            if h % 2 == 0:
                return lambda part: ou[:, part, k, half * HALF:(half + 1) * HALF]
            return lambda part: ht[:, part, 2 * k + half, HALF:T]

        def panel_part(h, part, c):
            if h % 2 == 0:
                x = ou[:, part, :, c * 256:(c + 1) * 256]
            else:
                at = HALF + (c % 2) * 256
                x = ht[:, part, c // 2::2, at:at + 256]
            return x.rearrange("p d (a t) -> p d a t", a=2)

        def later_pos(i):
            return i + ADA_FIRST + HEADS * HEAD_STREAM

        pieces = [slice(0, HALF), slice(HALF, T), slice(0, HALF), slice(HALF, 768), slice(768, T)]
        widths = [piece.stop - piece.start for piece in pieces]
        piece_cols = [slice(piece.start // P, piece.stop // P) for piece in pieces]
        piece_sums = [sums[u % 2][:, 0:width] for u, width in enumerate(widths)]

        def added(n):
            return KT + 7 * (n // KT) + n % KT + 1

        @block.sync
        def _(sp):
            def load(source, slot, p):
                sp.wait_ge(taken, p - STAGE_SLOTS + 1)
                sp.dma_start(stage[:, slot, :], source).then_inc(staged[slot], 16)

            sp.dma_start(vecs[:, :], vec).then_inc(consts_in, 16)
            sp.dma_start(ident[:, :], eye).then_inc(consts_in, 16)
            for p, (kind, a, b) in enumerate(START):
                if p == KT:
                    for k in range(KT):
                        sp.dma_start(xin[:, k, :], xT[k]).then_inc(x_in[k], 16)
                source = weights[a] if kind == "w" else ada[a, b]
                if p < STAGE_SLOTS:
                    sp.dma_start(stage[:, p, :], source).then_inc(staged[p], 16)
                else:
                    load(source, p % STAGE_SLOTS, p)
            with sp.Fori(0, HEADS) as h:
                sp.wait_ge(o_squared, h * TT + RING)
                sp.dma_start(trig[:, :, :], rope).then_inc(trig_in, 16)
                for idx, (kind, j) in enumerate(STREAM):
                    if idx == KT:
                        sp.wait_ge(row_scale, h * TT + 1)
                        sp.dma_start(hc[:, :], heads[h]).then_inc(hc_in, 16)
                    slot = (2 + idx) % STAGE_SLOTS
                    source = weights[h * HEAD_UNITS + j] if kind == "w" else ada[h + 2, j]
                    load(source, slot, head_pos(h, idx))
            for i in range(2, 16):
                if i == 4:
                    for a in range(2):
                        sp.wait_ge(stored[a], 16 * (1 + 4 * HEADS))
                if 4 <= i < 8:
                    for k in (2 * (i - 4), 2 * (i - 4) + 1):
                        sp.dma_start(x1[:, k, :], xT[k]).then_inc(x_in[k], 16)
                load(weights[W_OUT0 + i], i % STAGE_SLOTS, later_pos(i))
            for j in range(8):
                load(weights[W_MLP0 + j], j % STAGE_SLOTS, later_pos(16 + j))
            with sp.Fori(1, BLOCKS) as b:
                for j in range(8):
                    load(weights[b * 8 + (W_MLP0 + j)], j % STAGE_SLOTS, b * 8 + later_pos(16 + j))
            for n in range(3 * KT):
                piece, k = divmod(n, KT)
                part = pieces[2 + piece]
                sp.wait_ge(out_ready, n + 1)
                sp.dma_start(outT[k][:, part], x1[:, k, part]).then_inc(out_stored, 16)
            sp.wait_ge(out_stored, 16 * 3 * KT)

        @block.gpsimd
        def _(pool):
            pool.memset(power[:, :], -0.5).then_inc(setup_done, 1)
            pool.memset(ones[:, :], 1.0).then_inc(setup_done, 1)
            pool.wait_ge(setup_done, 2)

            def norm_power(n, cols):
                pool.wait_ge(z_done, n)
                pool.tensor_tensor(rcol[:, cols], zcol[:, cols], power[:, cols], ALU.pow).then_inc(pow_done, 1)

            norm_power(1, slice(0, KT))
            pool.wait_ge(rms_copied, 1)
            for k in range(KT):
                x_part = xin[:, k, HALF:T]
                pool.wait_ge(gained, k + 1)
                pool.tensor_tensor(x_part, x_part, rms_half, ALU.mult).then_inc(scaled_2, 1)
            with pool.Fori(0, HEADS) as h:
                for i in range(TT):
                    a = i % 2
                    pool.wait_ge(o_squared, h * TT + (RING + i + 1))
                    if i == 0:
                        pool.wait_ge(hc_in, h * 16 + 16)
                    pool.tensor_tensor(rs[:, 1, a:a + 1], rs[:, 0, a:a + 1], hc[:, H_EPS + a:H_EPS + a + 1], ALU.add)\
                        .then_inc(scale_step, 1)
                    pool.wait_ge(scale_step, h * TT + (i + 1))
                    pool.tensor_tensor(rs[:, 2, a:a + 1], rs[:, 1, a:a + 1], power[:, 0:1], ALU.pow).then_inc(row_scale, 1)
            for h in range(HEADS):
                for a in range(2):
                    pool.wait_ge(stored[a], 16 * (1 + 4 * (h + 1)))
                if h == 0:
                    pool.wait_ge(o_squared, RING + TT * HEADS)
                for c in range(4):
                    n = 4 * h + c
                    if n >= 2:
                        pool.wait_ge(o_taken, n - 1)
                    pool.dma_start(ostage[:, n % 2, :, :], gated_dram[h, 2 * c:2 * c + 2].rearrange("a p n -> p a n"))\
                        .then_inc(o_in[n % 2], 16)

            def add_square(n):
                u, m = divmod(n, KT)
                if m == KT - 1:
                    return
                pool.wait_ge(squared, KT + n + 1)
                squares = squares2[n % 2][:, 0:widths[u]]
                if m == 0:
                    if u == 4:
                        pool.wait_ge(bc_done, 5)
                    pool.tensor_copy(piece_sums[u], squares).then_inc(sq_added, 1)
                else:
                    pool.wait_ge(sq_added, added(n - 1))
                    pool.tensor_tensor(piece_sums[u], piece_sums[u], squares, ALU.add).then_inc(sq_added, 1)

            for n in range(5 * KT):
                if n and n % KT == 0:
                    norm_power(n // KT + 1, piece_cols[n // KT - 1])
                add_square(n)
            norm_power(6, piece_cols[4])

        @block.scalar
        def _(act):
            def split_hi(slot, split_slot, arrived):
                act.wait_ge(staged[slot], arrived)
                act.activation(wsplit[:, split_slot, 0, :], stage[:, slot, :], ACT.Copy).then_inc(hi_made, 1)

            def arrived(pos0):
                return 16 * (pos0 // STAGE_SLOTS + 1)

            def head_hi(h, j):
                if j in (2, 3, 4):
                    act.wait_ge(g_unit_free, h * 3 + (j - 1))
                elif j == 5:
                    act.wait_ge(g_done, h * TT + RING)
                elif j in (6, 7, 8, 9):
                    act.wait_ge(qk_done, h * TT + 2 * (j - 5))
                elif j in (10, 11, 12):
                    act.wait_ge(v_unit_free, h * 3 + (j - 9))
                else:
                    act.wait_ge(v_done, h * TT + TT)
                pos = unit_pos(0, j)
                split_hi(pos % STAGE_SLOTS, j % SPLIT_SLOTS, h * (16 * HEAD_STREAM // STAGE_SLOTS) + arrived(pos))

            def square_piece(n, count):
                u, m = divmod(n, KT)
                act.wait_ge(*count)
                if n >= 2 and (n - 2) % KT == KT - 1:
                    act.wait_ge(sums_done, 2 + (n - 2) // KT)
                elif n >= 2:
                    act.wait_ge(sq_added, added(n - 2))
                act.activation(squares2[n % 2][:, 0:widths[u]], x1[:, m, pieces[u]], ACT.Square).then_inc(squared, 1)

            def ht_write(n, source, shift, ready):
                half, k = divmod(n % 16, KT)
                act.wait_ge(*ready)
                act.activation(ht[:, 0, k, half * HALF:(half + 1) * HALF], source, ACT.Identity,
                               bias=mods[:, shift + k:shift + k + 1]).then_inc(ht_hi, 1)

            act.wait_ge(consts_in, 32)
            act.activation(cond[:, :], vecs[:, C_COND:C_COND + KT], ACT.Silu).then_inc(cond_done, 1)
            for k in range(KT):
                act.wait_ge(x_in[k], 16)
                if k >= 2:
                    act.wait_ge(sq_added, k - 1)
                act.activation(squares1[k % 2], xin[:, k, :], ACT.Square).then_inc(squared, 1)
            split_hi(0, 0, arrived(KT))
            act.wait_ge(gains_done, 1)
            for k in range(KT):
                act.activation(xin[:, k, HALF:T], xin[:, k, HALF:T], ACT.Copy, scale=gains[:, 0, k:k + 1]).then_inc(gained, 1)
            act.wait_ge(bc_done, 2)
            act.activation(rms_half, pa[1][:, :], ACT.Copy).then_inc(rms_copied, 1)
            act.wait_ge(mods_done, 2)
            for n in range(16):
                half, k = divmod(n, KT)
                ht_write(n, xin[:, k, half * HALF:(half + 1) * HALF], M_SH1,
                         (scaled_2, k + 1) if half else (scaled, k + 1))
                if n == KT:
                    split_hi(1, 1, arrived(ADA_FIRST + 1))

            def head(h, last):
                for j in range(2, 10):
                    head_hi(h, j)
                def values_hi(i):
                    act.wait_ge(v_done, h * TT + (i + 1))
                    act.activation(vs[:, 0, i, :], pp[i % 4][:, :], ACT.Copy).then_inc(v_hi, 1)

                def keys_hi(c):
                    act.wait_ge(kt_done, h * 3 + (c + 1))
                    if c:
                        act.wait_ge(kv_done, h * 3 + c)
                    for a in range(2):
                        last = act.activation(kn[:, 0, a, :], keys_bank[c][:, a * DK:(a + 1) * DK], ACT.Copy,
                                              scale=hc[:, H_ZETA + a:H_ZETA + a + 1])
                    last.then_inc(kn_hi, 1)

                def scores_hi(c):
                    act.wait_ge(sc_masked, h * NCHUNK + (c + 1))
                    if c:
                        act.wait_ge(o_done, h * TT + 2 * c)
                    act.activation(scs[:, 0, :], pa[c % 2][:, 0:384], ACT.Copy).then_inc(sc_hi, 1)

                def queries_hi(c):
                    act.activation(qs[:, 0], qk[:, 0:2, c * CHUNK:(c + 1) * CHUNK], ACT.Copy).then_inc(q_hi, 1)

                def state_hi_of(c):
                    act.wait_ge(state_new, h * 3 + (c + 1))
                    if c:
                        act.wait_ge(o_done, h * TT + 2 * (c + 1))
                    act.activation(sts[:, 0, :], state[:, :], ACT.Copy).then_inc(state_hi, 1)

                def square(i):
                    act.wait_ge(o_done, h * TT + (i + 1))
                    act.activation(output_tile(i), by_output(pa[2 + i % 2]), ACT.Square,
                                   accum_out=rs[:, 0, i % 2:i % 2 + 1]).then_inc(o_squared, 1)

                for i in range(TT - 1):
                    values_hi(i)
                act.wait_ge(hc_in, h * 16 + 16)
                keys_hi(0)
                scores_hi(0)
                queries_hi(1)
                values_hi(TT - 1)
                keys_hi(1)
                square(0)
                state_hi_of(0)
                square(1)
                scores_hi(1)
                head_hi(h, 10)
                keys_hi(2)
                square(2)
                square(3)
                scores_hi(2)
                queries_hi(2)
                state_hi_of(1)
                head_hi(h, 11)
                square(4)
                square(5)
                scores_hi(3)
                queries_hi(3)
                state_hi_of(2)
                head_hi(h, 12)
                square(6)
                square(7)
                head_hi(h, 13)

                def silu(i):
                    act.wait_ge(g_done, h * TT + (RING + i + 1))
                    act.activation(pp[i % 4][:, :], pp[i % 4][:, :], ACT.Silu).then_inc(silu_done, 1)

                def turned_out(i):
                    act.wait_ge(t_done, h * TT + (i + 1))
                    act.wait_ge(stored[i % 2], h * 64 + 16 * (i // 2 + 1))
                    act.activation(turned[:, i % 2, :], pa[i % 2][:, :], ACT.Copy).then_inc(t_read, 1)

                def store(i):
                    act.wait_ge(t_read, h * TT + (RING + i + 1))
                    act.dma_start(gated_dram[h, i], turned[:, i % 2, :]).then_inc(stored[i % 2], 16)

                silu(0)
                for i in range(1, TT):
                    silu(i)
                    turned_out(i - 1)
                    store(i - 1)
                    if last and 2 <= i < 6:
                        o_split_hi(i - 2)
                turned_out(TT - 1)
                store(TT - 1)

            def later_hi(i):
                if i in (2, 3):
                    act.wait_ge(g_unit_free, 3 * HEADS + i - 1)
                elif i >= 16:
                    act.wait_ge(wo_done, 56 + 2 * (i - 15))
                else:
                    act.wait_ge(wo_done, 4 * (i - 3))
                pos = later_pos(i)
                split_hi(pos % STAGE_SLOTS, i % FLOW_SLOTS, arrived(pos))

            def o_split_hi(n):
                h, c = divmod(n, 4)
                act.wait_ge(o_in[n % 2], 16 * (n // 2 + 1))
                if c == 0 and h == 1:
                    act.wait_ge(g_done, RING + TT * HEADS)
                if c == 0 and h >= 2:
                    act.wait_ge(wo_done, 16 * (h - 1))
                act.activation(panel_part(h, 0, c), ostage[:, n % 2, :, :].rearrange("p a (d t) -> p d a t", d=4),
                               ACT.Copy).then_inc(o_hi, 1)

            with act.Fori(0, HEADS - 1) as h:
                head(h, False)
            head(HEADS - 1, True)

            later_hi(2)
            later_hi(3)
            for h in range(HEADS - 1):
                for j in range(4):
                    o_split_hi(4 * h + 4 + j)
                    later_hi(4 * h + 4 + j)

            act.wait_ge(o_taken, 16)
            for n in range(16):
                if 10 <= n < 14:
                    for k in (2 * (n - 10), 2 * (n - 10) + 1):
                        ht_write(16 + k, scaled2[k % 2], M_SH2, (scaled, KT + k + 1))
                square_piece(n, (wo_read, 48 + n + 1))
                if n == 9:
                    later_hi(16)

            def hidden_hi(b, m, half, n):
                act.wait_ge(u_done, b * 8 + (n + 1))
                act.wait_ge(u_read, b * 8 + (RING + n - 1))
                act.activation(relu[n % 2], pp[n % 4][:, :], ACT.Relu).then_inc(relu_done, 1)
                act.wait_ge(relu_done, b * 8 + (n + 1))
                act.activation(ou[:, 0, m, half * HALF:(half + 1) * HALF], relu[n % 2], ACT.Square).then_inc(u_hi, 1)

            def mlp_hi(b, j, used=None):
                pos = later_pos(16 + j)
                if j < 4:
                    act.wait_ge(y_done, (b - 1) * 16 + 4 * (j + 1))
                else:
                    act.wait_ge(u_done, b * 8 + (used or 2 * (j - 3)))
                split_hi(pos % STAGE_SLOTS, j % FLOW_SLOTS, b * 32 + arrived(pos))

            later_hi(17)
            hidden_hi(0, 0, 0, 0)
            later_hi(18)
            later_hi(19)
            act.wait_ge(bc_done, 4)
            hidden_hi(0, 1, 0, 1)
            for k in range(KT):
                ht_write(24 + k, scaled2[k % 2], M_SH2, (scaled, 2 * KT + k + 1))
            for n in range(2, 8):
                half, m = divmod(n, 4)
                hidden_hi(0, m, half, n)
                if half:
                    mlp_hi(0, 4 + m, 4 + m + 1)
            for j in range(4):
                mlp_hi(1, j)
            with act.Fori(1, BLOCKS - 1) as b:
                for n in range(8):
                    m, half = divmod(n, 2)
                    hidden_hi(b, m, half, n)
                    if half:
                        mlp_hi(b, 4 + m)
                for j in range(4):
                    mlp_hi(b + 1, j)
            for n in range(8):
                m, half = divmod(n, 2)
                hidden_hi(BLOCKS - 1, m, half, n)
                if half:
                    mlp_hi(BLOCKS - 1, 4 + m)

            for n in range(3 * KT):
                square_piece(16 + n, (y_read, 4 + 16 * (BLOCKS - 1) + n + 1))

        @block.vector
        def _(dve):
            vec_ = nc.vector

            def split_lo(slot, split_slot, made):
                dve.wait_ge(hi_made, made)
                vec_.tensor_tensor(wsplit[:, split_slot, 1, :], stage[:, slot, :], wsplit[:, split_slot, 0, :].bitcast(F32),
                                   ALU.subtract).then_inc(taken, 1)

            def head_lo(h, j):
                split_lo(unit_pos(0, j) % STAGE_SLOTS, j % SPLIT_SLOTS, h * HEAD_UNITS + (j + 1))

            def ada_step(k, slot, arrived, pos):
                dve.wait_ge(staged[slot], arrived)
                if k == 0:
                    vec_.tensor_scalar(ada_sum, stage[:, slot, :], cond[:, 0:1], None, ALU.mult).then_inc(taken, 1)
                else:
                    dve.wait_ge(taken, pos)
                    vec_.scalar_tensor_tensor(ada_sum, stage[:, slot, :], cond[:, k:k + 1], ada_sum,
                                              ALU.mult, ALU.add).then_inc(taken, 1)

            def mean_square(n, cols, bank, sums_count):
                dve.wait_ge(sums_done, sums_count)
                width = cols.stop - cols.start
                vec_.tensor_scalar(zcol[:, cols], bank[:, 0:width], 1.0 / D, EPS, ALU.mult, ALU.add).then_inc(z_done, 1)

            def diagonal(n, cols, out):
                dve.wait_ge(pow_done, n)
                width = cols.stop - cols.start
                vec_.tensor_tensor(out.rearrange("p (a t) -> p a t", t=P),
                                   ident[:, :].unsqueeze(1).to_broadcast([P, width, P]),
                                   rcol[:, cols].unsqueeze(2).to_broadcast([P, width, P]), ALU.mult).then_inc(diag_done, 1)

            def half_cols(half):
                return slice(4 * half, 4 * half + 4)

            def ht_lo(n, source, shift):
                half, k = divmod(n % 16, KT)
                part = slice(half * HALF, (half + 1) * HALF)
                dve.wait_ge(ht_hi, n + 1)
                vec_.scalar_tensor_tensor(ht[:, 1, k, part], source, mods[:, shift + k:shift + k + 1],
                                          ht[:, 0, k, part].bitcast(F32), ALU.add, ALU.subtract).then_inc(ht_done, 1)

            dve.wait_ge(cond_done, 1)
            for k in range(KT):
                ada_step(k, k % STAGE_SLOTS, 16 * (k // STAGE_SLOTS + 1), k)
            for k in range(KT):
                dve.wait_ge(squared, k + 1)
                if k == 0:
                    vec_.tensor_copy(sums1, squares1[0]).then_inc(sq_added, 1)
                else:
                    dve.wait_ge(sq_added, k)
                    vec_.tensor_tensor(sums1, sums1, squares1[k % 2], ALU.add).then_inc(sq_added, 1)
            dve.wait_ge(ada_done, 1)
            vec_.tensor_tensor(mods[:, M_SC1:M_SC1 + KT], pp[0][:, 0:8],
                               vecs[:, C_ADAB + M_SC1:C_ADAB + M_SC1 + KT], ALU.add).then_inc(mods_done, 1)
            dve.wait_ge(mods_done, 1)
            vec_.scalar_tensor_tensor(gains[:, 0, :], mods[:, M_SC1:M_SC1 + KT], 1.0, vecs[:, C_GMIX:C_GMIX + KT],
                                      ALU.add, ALU.mult).then_inc(gains_done, 1)

            def sh1_step(k):
                pos = KT + 1 + k
                ada_step(k, pos % STAGE_SLOTS, 16 * (pos // STAGE_SLOTS + 1), pos)

            def prescale(n):
                half, k = divmod(n, KT)
                x_part = xin[:, k, half * HALF:(half + 1) * HALF]
                if k == 0:
                    dve.wait_ge(bc_done, half + 1)
                vec_.scalar_tensor_tensor(x_part, x_part, gains[:, 0, k:k + 1], pa[half][:, :], ALU.mult, ALU.mult)\
                    .then_inc(scaled, 1)

            split_lo(0, 0, 1)
            sh1_step(0)
            mean_square(1, slice(0, KT), pa[2], 1)
            sh1_step(1)
            diagonal(1, slice(0, KT), diag1)
            sh1_step(2)
            for n in range(KT):
                if 3 + n < SH1_SPLIT:
                    sh1_step(3 + n)
                prescale(n)
            dve.wait_ge(taken, 2 * KT + 1)
            vec_.tensor_tensor(mods[:, M_SH1:M_SH1 + KT], pp[1][:, 0:8],
                               vecs[:, C_ADAB + M_SH1:C_ADAB + M_SH1 + KT], ALU.add).then_inc(mods_done, 1)
            dve.wait_ge(mods_done, 2)
            for n in range(16):
                half, k = divmod(n, KT)
                ht_lo(n, xin[:, k, half * HALF:(half + 1) * HALF], M_SH1)
                if n == KT:
                    split_lo(1, 1, 2)

            def head(h, last):
                for j in range(2, 6):
                    head_lo(h, j)
                dve.wait_ge(trig_in, h * 16 + 16)
                dve.wait_ge(t_read, h * TT + RING)
                for n in range(8):
                    m, half = divmod(n, 2)
                    part = slice(half * HALF, (half + 1) * HALF)
                    cos, sin = trig[:, 0, part], trig[:, 1, part]
                    psum = pp[n % 4][:, :]
                    dve.wait_ge(qk_done, h * 8 + (n + 1))
                    if m % 2 == 0:
                        vec_.tensor_tensor(qk[:, m, part], psum, cos, ALU.mult)
                        vec_.tensor_tensor(qk[:, m + 1, part], psum, sin, ALU.mult).then_inc(qk_read, 1)
                    else:
                        t1, t2 = rope_tmp[:, 2 * half, :], rope_tmp[:, 2 * half + 1, :]
                        vec_.tensor_tensor(t1, psum, sin, ALU.mult)
                        vec_.tensor_tensor(t2, psum, cos, ALU.mult).then_inc(qk_read, 1)
                        dve.wait_ge(qk_read, h * 8 + (n + 1))
                        vec_.tensor_tensor(qk[:, m - 1, part], qk[:, m - 1, part], t1, ALU.subtract)
                        vec_.tensor_tensor(qk[:, m, part], qk[:, m, part], t2, ALU.add).then_inc(roped, 1)
                    if half == 1:
                        head_lo(h, 6 + m)

                for a in range(2):
                    dve.wait_ge(stored[a], h * 64 + 16)
                dve.wait_ge(roped, h * 4 + 4)
                def values_lo(i):
                    dve.wait_ge(v_hi, h * TT + (i + 1))
                    vec_.tensor_tensor(vs[:, 1, i, :], pp[i % 4][:, :], vs[:, 0, i, :].bitcast(F32), ALU.subtract)\
                        .then_inc(v_read, 1)

                for k in range(KT):
                    pos = head_pos(0, KT + k)
                    ada_step(k, pos % STAGE_SLOTS, h * (16 * HEAD_STREAM // STAGE_SLOTS) + 16 * (pos // STAGE_SLOTS + 1),
                             head_pos(h, KT + k))
                    if k < TT - 1:
                        values_lo(k)

                def mask(c):
                    dve.wait_ge(sc_done, h * NCHUNK + (c + 1))
                    vec_.tensor_tensor(pa[c % 2][:, 0:384], pa[c % 2][:, 0:384], hc[:, H_MASK:H_MASK + 384], ALU.mult)\
                        .then_inc(sc_masked, 1)

                def scores_lo(c):
                    dve.wait_ge(sc_masked, h * NCHUNK + (c + 1))
                    dve.wait_ge(sc_hi, h * NCHUNK + (c + 1))
                    vec_.tensor_tensor(scs[:, 1, :], pa[c % 2][:, 0:384], scs[:, 0, :].bitcast(F32), ALU.subtract)\
                        .then_inc(sc_read, 1)

                def keys_lo(c):
                    dve.wait_ge(kn_hi, h * 3 + (c + 1))
                    for a in range(2):
                        last = vec_.scalar_tensor_tensor(kn[:, 1, a, :], keys_bank[c][:, a * DK:(a + 1) * DK],
                                                         hc[:, H_ZETA + a:H_ZETA + a + 1], kn[:, 0, a, :].bitcast(F32),
                                                         ALU.mult, ALU.subtract)
                    last.then_inc(kt_read, 1)

                def queries_lo(c):
                    dve.wait_ge(q_hi, h * 3 + c)
                    vec_.tensor_tensor(qs[:, 1], qk[:, 0:2, c * CHUNK:(c + 1) * CHUNK], qs[:, 0].bitcast(F32),
                                       ALU.subtract).then_inc(q_split, 1)

                def new_state(c):
                    dve.wait_ge(kv_done, h * 3 + (c + 1))
                    if c:
                        dve.wait_ge(state_new, h * 3 + c)
                        dve.wait_ge(state_done, h * 3 + c)
                    for a in range(2):
                        part = state[:, a * DV:(a + 1) * DV]
                        if c == 0:
                            last = vec_.tensor_copy(part, pp[a][:, :])
                        else:
                            last = vec_.scalar_tensor_tensor(part, part, hc[:, H_DECAY:H_DECAY + 1], pp[a][:, :],
                                                             ALU.mult, ALU.add)
                    last.then_inc(state_new, 1)

                def state_lo(c):
                    dve.wait_ge(state_new, h * 3 + (c + 1))
                    dve.wait_ge(state_hi, h * 3 + (c + 1))
                    vec_.tensor_tensor(sts[:, 1, :], state[:, :], sts[:, 0, :].bitcast(F32), ALU.subtract).then_inc(state_done, 1)

                def normalise(i):
                    dve.wait_ge(row_scale, h * TT + (i + 2))
                    vec_.tensor_scalar(output_tile(i), by_output(pa[2 + i % 2]), rs[:, 2, i % 2:i % 2 + 1], math.sqrt(DV),
                                       ALU.mult, ALU.mult)\
                        .then_inc(o_read, 1)

                dve.wait_ge(hc_in, h * 16 + 16)
                mask(0)
                keys_lo(0)
                mask(1)
                scores_lo(0)
                queries_lo(1)
                dve.wait_ge(ada_done, h + 2)
                vec_.tensor_tensor(mods[:, bass.ds(h * 8 + 16, 8)], pa[2][:, 0:8],
                                   vecs[:, bass.ds(h * 8 + (C_ADAB + 16), 8)], ALU.add).then_inc(mods_done, 1)
                values_lo(TT - 1)
                new_state(0)
                keys_lo(1)
                state_lo(0)
                normalise(0)
                normalise(1)
                scores_lo(1)
                new_state(1)
                mask(2)
                head_lo(h, 10)
                keys_lo(2)
                normalise(2)
                scores_lo(2)
                queries_lo(2)
                state_lo(1)
                normalise(3)
                new_state(2)
                mask(3)
                head_lo(h, 11)
                normalise(4)
                scores_lo(3)
                queries_lo(3)
                state_lo(2)
                normalise(5)
                head_lo(h, 12)
                normalise(6)
                normalise(7)
                head_lo(h, 13)
                dve.wait_ge(o_read, h * TT + (2 + TT))
                for i in range(TT):
                    dve.wait_ge(silu_done, h * TT + (i + 1))
                    vec_.tensor_tensor(output_tile(i), output_tile(i), by_output(pp[i % 4]), ALU.mult).then_inc(gated, 1)
                    if last and 2 <= i < 6:
                        o_split_lo(i - 2)

            def o_split_lo(n):
                h, c = divmod(n, 4)
                dve.wait_ge(o_hi, n + 1)
                vec_.tensor_tensor(panel_part(h, 1, c), ostage[:, n % 2, :, :].rearrange("p a (d t) -> p d a t", d=4),
                                   panel_part(h, 0, c).bitcast(F32), ALU.subtract).then_inc(o_taken, 1)

            with dve.Fori(0, HEADS - 1) as h:
                head(h, False)
            head(HEADS - 1, True)

            dve.wait_ge(mods_done, 6)
            vec_.tensor_scalar(gains[:, 1, :], mods[:, M_GT1:M_GT1 + KT], 1.0, None, ALU.add)
            vec_.tensor_scalar(gains[:, 2, :], mods[:, M_GT2:M_GT2 + KT], 1.0, None, ALU.add)
            vec_.scalar_tensor_tensor(gains[:, 3, :], mods[:, M_SC2:M_SC2 + KT], 1.0, vecs[:, C_GMLP:C_GMLP + KT],
                                      ALU.add, ALU.mult).then_inc(gains_done, 1)
            dve.wait_ge(gains_done, 2)

            def later_lo(i):
                split_lo(later_pos(i) % STAGE_SLOTS, i % FLOW_SLOTS, W_OUT0 + i + 1)

            def residual(m, piece, psum, gate, read):
                part = pieces[piece]
                vec_.scalar_tensor_tensor(x1[:, m, part], psum[:, 0:widths[piece]], gains[:, gate, m:m + 1], x1[:, m, part],
                                          ALU.mult, ALU.add).then_inc(read, 1)

            later_lo(2)
            later_lo(3)
            for h in range(HEADS - 1):
                for j in range(4):
                    for g in range(4 * j, 4 * j + 4):
                        m, half = divmod(g, 2)
                        if h == 0:
                            dve.wait_ge(x_in[m], 32)
                        dve.wait_ge(wo_done, 16 * h + g + 1)
                        residual(m, half, pp[g % 4], 1, wo_read)
                        if g % 4 == 1:
                            o_split_lo(4 * h + 4 + j)
                    later_lo(4 * h + 4 + j)

            def scale(n):
                half, k = divmod(n, KT)
                if k == 0:
                    dve.wait_ge(bc_done, 2 + half + 1)
                if n >= 2:
                    dve.wait_ge(ht_done, 16 + n - 1)
                vec_.scalar_tensor_tensor(scaled2[n % 2], x1[:, k, half * HALF:(half + 1) * HALF],
                                          gains[:, 3, k:k + 1], pa[half][:, :], ALU.mult, ALU.mult).then_inc(scaled, 1)

            for n in range(16):
                half, m = divmod(n, KT)
                if n == 9:
                    mean_square(2, half_cols(0), pa[2], 2)
                    diagonal(2, half_cols(0), sums[0])
                if 10 <= n < 14:
                    for k in (2 * (n - 10), 2 * (n - 10) + 1):
                        scale(k)
                        if k:
                            ht_lo(16 + k - 1, scaled2[(k - 1) % 2], M_SH2)
                if n == 14:
                    ht_lo(16 + 7, scaled2[1], M_SH2)
                dve.wait_ge(wo_done, 48 + n + 1)
                residual(m, half, pp[n % 4], 1, wo_read)
                if n == 9:
                    later_lo(16)

            def hidden_lo(b, m, half, n):
                psum = pp[n % 4][:, :]
                part = slice(half * HALF, (half + 1) * HALF)
                dve.wait_ge(relu_done, b * 8 + (n + 1))
                vec_.scalar_tensor_tensor(psum, psum, 0.0, relu[n % 2], ALU.max, ALU.mult).then_inc(u_sq, 1)
                dve.wait_ge(u_hi, b * 8 + (n + 1))
                dve.wait_ge(u_sq, b * 8 + (n + 1))
                vec_.tensor_tensor(ou[:, 1, m, part], psum, ou[:, 0, m, part].bitcast(F32), ALU.subtract).then_inc(u_read, 1)

            def mlp_lo(b, j):
                split_lo(later_pos(16 + j) % STAGE_SLOTS, j % FLOW_SLOTS, b * 8 + (W_MLP0 + j + 1))

            def outputs(b):
                for g in range(16):
                    m, half = divmod(g, 2)
                    dve.wait_ge(y_done, b * 16 + (g + 1))
                    residual(m, half, pa[g % 4], 2, y_read)
                    if g % 4 == 3:
                        mlp_lo(b + 1, g // 4)

            later_lo(17)
            mean_square(3, half_cols(1), pa[3], 3)
            hidden_lo(0, 0, 0, 0)
            later_lo(18)
            later_lo(19)
            diagonal(3, half_cols(1), sums[1])
            hidden_lo(0, 1, 0, 1)
            for n in range(KT, 16):
                scale(n)
                if n > KT:
                    ht_lo(16 + n - 1, scaled2[(n - 1) % 2], M_SH2)
            ht_lo(31, scaled2[1], M_SH2)
            for n in range(2, 8):
                half, m = divmod(n, 4)
                hidden_lo(0, m, half, n)
                if half:
                    mlp_lo(0, 4 + m)
            outputs(0)
            with dve.Fori(1, BLOCKS - 1) as b:
                for n in range(8):
                    m, half = divmod(n, 2)
                    hidden_lo(b, m, half, n)
                    if half:
                        mlp_lo(b, 4 + m)
                outputs(b)
            for n in range(8):
                m, half = divmod(n, 2)
                hidden_lo(BLOCKS - 1, m, half, n)
                if half:
                    mlp_lo(BLOCKS - 1, 4 + m)

            def final(n):
                piece, k = divmod(n, KT)
                tile = x1[:, k, pieces[2 + piece]]
                if k == 0:
                    dve.wait_ge(bc_done, 5 + piece)
                vec_.scalar_tensor_tensor(tile, tile, vecs[:, C_GFIN + k:C_GFIN + k + 1],
                                          pp[piece % 2][:, 0:widths[2 + piece]], ALU.mult, ALU.mult).then_inc(out_ready, 1)

            def final_rms(piece):
                mean_square(4 + piece, piece_cols[2 + piece], pp[2 + piece % 2], 4 + piece)
                diagonal(4 + piece, piece_cols[2 + piece], piece_sums[2 + piece])

            for n in range(3 * KT):
                piece, m = divmod(n, KT)
                if n in (KT + 1, 2 * KT + 1):
                    final_rms(piece - 1)
                if 12 <= n < 20:
                    final(n - 12)
                if 20 <= n:
                    final(KT + 2 * (n - 20))
                    final(KT + 2 * (n - 20) + 1)
                dve.wait_ge(y_done, 16 * (BLOCKS - 1) + n + 1)
                residual(m, 2 + piece, pa[n % 4], 2, y_read)
            final_rms(2)
            for n in range(2 * KT, 3 * KT):
                final(n)

        @block.tensor
        def _(pe):
            mm = nc.tensor.matmul

            def product(out, stationary, moving, start, stop):
                mm(out, stationary(0), moving(0), start=start, stop=False)
                mm(out, stationary(0), moving(1), start=False, stop=False)
                return mm(out, stationary(1), moving(0), start=False, stop=stop)

            def by_feature(slot, tile):
                return lambda part: wsplit[:, slot, part, tile * P:(tile + 1) * P]

            def half_of(x, k, half):
                return lambda part: x[:, part, k, half * HALF:(half + 1) * HALF]

            def token_sums(sq, columns, bank, first, last):
                for j in range(columns):
                    done = mm(bank[:, j:j + 1], sq[:, j * P:(j + 1) * P], ones[:, 0:1],
                              start=first and j == 0, stop=last, skip_group_check=True)
                if last:
                    done.then_inc(sums_done, 1)

            def piece_totals(u, bank):
                columns = widths[u] // P
                pe.wait_ge(sq_added, added(KT * u + KT - 2))
                token_sums(piece_sums[u], columns, bank, True, False)
                pe.wait_ge(squared, KT + KT * (u + 1))
                token_sums(squares2[1], columns, bank, False, True)

            def broadcast(bank, diag):
                mm(bank[:, 0:diag.shape[-1]], ones[:, :], diag, start=True, stop=True).then_inc(bc_done, 1)

            def ada_total(bank, column, acc):
                for m in range(KT):
                    last = mm(bank[:, column + m:column + m + 1], acc[:, m * P:(m + 1) * P], ones[:, 0:1],
                              start=True, stop=True)
                last.then_inc(ada_done, 1)

            pe.sem_inc(g_unit_free, 3)
            pe.sem_inc(g_done, RING)
            pe.sem_inc(gated, RING)
            pe.sem_inc(o_squared, RING)
            pe.sem_inc(o_read, 2)
            pe.sem_inc(t_read, RING)
            pe.sem_inc(row_scale, 1)
            pe.sem_inc(stored[0], 16)
            pe.sem_inc(stored[1], 16)
            pe.sem_inc(u_read, RING)
            pe.sem_inc(y_read, 4)

            pe.wait_ge(setup_done, 2)
            def keep_warm(n):
                for _ in range(n):
                    mm(pa[3][:, 0:P], ones[:, :], ones[:, :], start=True, stop=True)

            pe.wait_ge(taken, KT)
            ada_total(pp[0], 0, ada_sum)
            keep_warm(30)
            pe.wait_ge(sq_added, KT)
            token_sums(sums1, TT, pa[2], True, True)
            keep_warm(8)
            pe.wait_ge(diag_done, 1)
            for half in range(2):
                broadcast(pa[half], diag1[:, half * HALF:(half + 1) * HALF])
            keep_warm(30)
            for k in range(SH1_SPLIT - 1, KT):
                pos = KT + 1 + k
                if k == SH1_SPLIT - 1:
                    pe.wait_ge(taken, pos + 1)
                else:
                    pe.wait_ge(staged[pos % STAGE_SLOTS], 16 * (pos // STAGE_SLOTS + 1))
                for m in range(KT):
                    part = slice(m * P, (m + 1) * P)
                    stationary, moving = (ada_sum[:, part], ones[:, 0:1]) if k == SH1_SPLIT - 1 else \
                        (stage[:, pos % STAGE_SLOTS, part], cond[:, k:k + 1])
                    last = mm(pp[1][:, m:m + 1], stationary, moving, start=k == SH1_SPLIT - 1 and m == 0, stop=k == KT - 1,
                              skip_group_check=True)
                if k >= SH1_SPLIT:
                    last.then_inc(taken, 1)

            def rotated(h, n):
                m, half = divmod(n, 2)
                if half == 0:
                    pe.wait_ge(taken, unit_pos(h, m) + 1)
                if n < 4:
                    pe.wait_ge(gated, h * TT + (5 + n))
                else:
                    pe.wait_ge(qk_read, h * TT + (n - 3))
                for k in range(KT):
                    if m == 0:
                        pe.wait_ge(ht_done, 8 * half + k + 1)
                    last = product(pp[n % 4][:, :], by_feature(m, k), half_of(ht, k, half), k == 0, k == KT - 1)
                last.then_inc(qk_done, 1)

            def head(h, meanwhile):
                for n in range(1, 8):
                    rotated(h, n)

                def token_panel(i, first_unit, free):
                    for k in range(KT):
                        u, slot = divmod(k, 2)[0], (first_unit + k // 2) % SPLIT_SLOTS
                        last = product(pp[i % 4][:, :], lambda part: ht[:, part, k, i * P:(i + 1) * P],
                                       lambda part: wsplit[:, slot, part, (k % 2) * DV:(k % 2 + 1) * DV], k == 0, k == KT - 1)
                        if i == TT - 1 and k in (1, 3, 5):
                            last.then_inc(free, 1)
                    return last

                def values(i):
                    if i == 0:
                        pe.wait_ge(taken, unit_pos(h, 7) + 1)
                    if i < 4:
                        pe.wait_ge(qk_read, h * TT + (5 + i))
                    else:
                        pe.wait_ge(v_read, h * TT + (i - 3))
                    token_panel(i, 4, v_unit_free).then_inc(v_done, 1)

                def scores(c):
                    if c < 2:
                        pe.wait_ge(t_read, h * TT + RING)
                    else:
                        pe.wait_ge(sc_read, h * NCHUNK + (c - 1))
                    t0 = c * CHUNK
                    for a in range(2):
                        mm(pa[c % 2][:, 0:256], qk[:, 2 + a, t0:t0 + P], qk[:, a, t0:t0 + 256], start=a == 0, stop=a == 1)
                    for a in range(2):
                        last = mm(pa[c % 2][:, 256:384], qk[:, 2 + a, t0 + P:t0 + 256], qk[:, a, t0 + P:t0 + 256],
                                  start=a == 0, stop=a == 1)
                    last.then_inc(sc_done, 1)

                def keys(c):
                    if c == 0:
                        pe.wait_ge(o_read, h * TT + 2)
                    else:
                        pe.wait_ge(v_read, h * TT + (6 + c))
                    for s in range(2):
                        for a in range(2):
                            col = s * DK + a * P
                            t0 = c * CHUNK + s * P
                            last = nc.tensor.transpose(keys_bank[c][:, col:col + P], qk[:, 2 + a, t0:t0 + P], ident[:, :])
                    last.then_inc(kt_done, 1)

                def keys_values(c):
                    if c == 0:
                        pe.wait_ge(v_read, h * TT + 6)
                    else:
                        pe.wait_ge(state_new, h * 3 + c)
                    pe.wait_ge(kt_read, h * 3 + (c + 1))
                    for a in range(2):
                        for s in range(2):
                            last = product(pp[a][:, :], lambda part: kn[:, part, s, a * P:(a + 1) * P],
                                           lambda part: vs[:, part, 2 * c + s, :], s == 0, s == 1)
                    last.then_inc(kv_done, 1)

                def outputs(i):
                    c, par = divmod(i, 2)
                    pe.wait_ge(o_read, h * TT + (i + 1))
                    if i == 0:
                        pe.wait_ge(mods_done, h + 3)
                    pe.wait_ge(sc_read, h * NCHUNK + (c + 1))
                    pairs = [(scs[:, :, (s + par) * P:(s + par + 1) * P], vs[:, :, 2 * c + s, :]) for s in range(par + 1)]
                    if c:
                        pe.wait_ge(q_split, h * 3 + c)
                        pe.wait_ge(state_done, h * 3 + c)
                        pairs += [(qs[:, :, a, par * P:(par + 1) * P], sts[:, :, a * DV:(a + 1) * DV]) for a in range(2)]
                    for n, (stationary, moving) in enumerate(pairs):
                        last = product(pa[2 + par][:, :], lambda part: stationary[:, part], lambda part: moving[:, part],
                                       n == 0, n == len(pairs) - 1)
                    last.then_inc(o_done, 1)

                for i in range(TT - 1):
                    values(i)
                pe.wait_ge(roped, h * 4 + 4)
                scores(0)
                keys(0)
                scores(1)
                pe.wait_ge(taken, head_pos(h, KT + KT - 1) + 1)
                ada_total(pa[2], 0, ada_sum)
                values(TT - 1)
                keys(1)
                keys_values(0)
                outputs(0)
                outputs(1)
                scores(2)
                keys(2)
                keys_values(1)
                outputs(2)
                outputs(3)
                keys_values(2)
                scores(3)
                outputs(4)
                outputs(5)

                def turn(i):
                    if i < 2:
                        pe.wait_ge(sc_read, h * NCHUNK + (3 + i))
                    else:
                        pe.wait_ge(t_read, h * TT + (RING + i - 1))
                    pe.wait_ge(gated, h * TT + (RING + i + 1))
                    for d in range(4):
                        last = nc.tensor.transpose(pa[i % 2][:, d * P:(d + 1) * P], output_tile(i)[:, d], ident[:, :])
                    last.then_inc(t_done, 1)

                pe.wait_ge(taken, unit_pos(h, 11) + 1)
                for i in range(TT):
                    if i == 0:
                        pe.wait_ge(state_new, h * 3 + 3)
                    if i >= 4:
                        pe.wait_ge(gated, h * TT + (RING + i - 3))
                    token_panel(i, 8, g_unit_free).then_inc(g_done, 1)
                    if i == 0:
                        outputs(6)
                        outputs(7)
                    else:
                        turn(i - 1)
                meanwhile()
                turn(TT - 1)

            def panel_tile(h, g):
                m, half = divmod(g, 2) if h < 3 else divmod(g, KT)[::-1]
                if h == 0 and g < 4:
                    pe.wait_ge(gated, TT * HEADS + 5 + g)
                else:
                    pe.wait_ge(wo_read, 16 * h + g - 3)
                if m == 0:
                    pe.wait_ge(o_taken, 4 * h + 2 * (half + 1))
                if m % 2 == 0 and half == 0:
                    pe.wait_ge(taken, later_pos(4 * h + m // 2) + 1)
                for k in range(4):
                    last = product(pp[g % 4][:, :], by_feature(m // 2, (m % 2) * 4 + k), panel_half(h, k, half),
                                   k == 0, k == 3)
                last.then_inc(wo_done, 1)

            rotated(0, 0)
            with pe.Fori(0, HEADS - 1) as h:
                head(h, lambda: rotated(h + 1, 0))
            head(HEADS - 1, lambda: panel_tile(0, 0))

            for h in range(HEADS):
                for g in range(16):
                    if (h, g) != (0, 0):
                        panel_tile(h, g)
                    if h == 3 and g == 8:
                        piece_totals(0, pa[2])
                    if h == 3 and g == 9:
                        pe.wait_ge(diag_done, 2)
                        broadcast(pa[0], sums[0])

            def hidden(b, m, half, n, new_unit):
                if new_unit:
                    pe.wait_ge(taken, b * 8 + (later_pos(16 + m) + 1))
                pe.wait_ge(u_read, b * 8 + (RING + n - 3))
                for k in range(KT):
                    if m == 0:
                        pe.wait_ge(ht_done, 16 + 8 * half + k + 1)
                    last = product(pp[n % 4][:, :], by_feature(m, k), half_of(ht, k, half), k == 0, k == KT - 1)
                last.then_inc(u_done, 1)

            def second(b, m, piece, n, ks, wait):
                tokens = pieces[piece]
                for k in ks:
                    if wait:
                        pe.wait_ge(u_read, b * 8 + (RING + 2 * k + (tokens.start >= HALF) + 1))
                    last = product(pa[n % 4][:, 0:widths[piece]], by_feature(m // 2, (m % 2) * 4 + k),
                                   lambda part: ou[:, part, k, tokens], k == 0, k == 3)
                return last

            def outputs(b, order, after=None):
                for n, (m, piece) in enumerate(order):
                    if m % 2 == 0 and pieces[piece].start == 0:
                        pe.wait_ge(taken, b * 8 + (later_pos(16 + 4 + m // 2) + 1))
                    pe.wait_ge(y_read, b * 16 + (n + 1))
                    if n < 4:
                        second(b, m, piece, n, range(3), True)
                        if n == 3:
                            for n2, (m2, piece2) in enumerate(order[:4]):
                                second(b, m2, piece2, n2, [3], True).then_inc(y_done, 1)
                    else:
                        second(b, m, piece, n, range(4), n == KT).then_inc(y_done, 1)
                    if after:
                        after(n)

            by_tile = [(m, half) for m in range(KT) for half in range(2)]
            by_piece = [(m, piece) for piece in (2, 3, 4) for m in range(KT)]

            for n in range(8):
                half, m = divmod(n, 4)
                if n < 4:
                    pe.wait_ge(wo_read, 61 + n)
                hidden(0, m, half, n, half == 0)
                if n == 0:
                    piece_totals(1, pa[3])
                if n == 1:
                    pe.wait_ge(diag_done, 3)
                    broadcast(pa[1], sums[1])
            pe.wait_ge(u_read, RING + 7)
            outputs(0, by_tile)
            with pe.Fori(1, BLOCKS - 1) as b:
                for n in range(8):
                    m, half = divmod(n, 2)
                    hidden(b, m, half, n, half == 0)
                outputs(b, by_tile)
            for n in range(8):
                m, half = divmod(n, 2)
                hidden(BLOCKS - 1, m, half, n, half == 0)

            def final_totals(piece):
                piece_totals(2 + piece, pp[2 + piece % 2])

            def final_broadcast(piece):
                pe.wait_ge(diag_done, 4 + piece)
                broadcast(pp[piece % 2], piece_sums[2 + piece])

            def final_norm(n):
                if n in (KT, 2 * KT):
                    final_totals(n // KT - 1)
                if n in (KT + 2, 2 * KT + 2):
                    final_broadcast(n // KT - 1)
            outputs(BLOCKS - 1, by_piece, final_norm)
            final_totals(2)
            final_broadcast(2)



def kernel(**inputs):
    import numpy as _np
    import concourse.bacc as _bacc
    from concourse import mybir as _mybir
    from concourse.bass_utils import run_bass_kernel_spmd as _run

    f = {k: _np.asarray(a) for k, a in inputs.items()}

    def columns(a):
        return a.reshape(-1, P).T

    def rows(a):
        return a.reshape(-1, P, a.shape[-1])

    w_in = f["ret_w_in"][0]
    q, k, val, gate = (w_in[:, a:b] for a, b in ((0, D), (D, 2 * D), (2 * D, 4 * D), (4 * D, 6 * D)))
    units = []
    for h in range(HEADS):
        for m in (q, k):
            part = rows(m)[:, :, h * DK:(h + 1) * DK]
            for odd in range(2):
                units.append(part[:, :, odd::2].transpose(1, 0, 2).reshape(P, UNIT))
        for m in (val, gate):
            part = rows(m)[:, :, h * DV:(h + 1) * DV]
            for j in range(4):
                units.append(part[2 * j:2 * j + 2].transpose(1, 0, 2).reshape(P, UNIT))

    def panel(w):
        r = w.reshape(4, P, 4, 2, P).transpose(2, 1, 3, 0, 4)
        return [r[j].reshape(P, UNIT) for j in range(4)]

    for h in range(HEADS):
        units += panel(f["ret_w_out"][0][h * DV:(h + 1) * DV])
    for b in range(BLOCKS):
        w1 = rows(f["mlp_w1"][0])[:, :, b * HALF:(b + 1) * HALF]
        units += [w1[:, :, m * P:(m + 1) * P].transpose(1, 0, 2).reshape(P, UNIT) for m in range(4)]
        units += panel(f["mlp_w2"][0][b * HALF:(b + 1) * HALF])

    vec = _np.concatenate([columns(a) for a in (f["c"][0], f["ada_b"][0], f["norm_mix_g"][0], f["norm_mlp_g"][0],
                                                f["final_norm_g"])], axis=1)
    rope, heads, eye = constants()
    arrays = {
        "xT": f["x"][0].T.reshape(KT, P, T),
        "vec": vec,
        "ada": f["ada_w"][0].reshape(KT, P, 6, D).transpose(2, 0, 1, 3),
        "weights": _np.stack(units),
        "rope": rope, "heads": heads, "eye": eye,
    }
    arrays = {name: _np.ascontiguousarray(a) for name, a in arrays.items()}
    nc = _bacc.Bacc("TRN2", target_bir_lowering=False, num_devices=1)
    args = [nc.dram_tensor(name, a.shape, _mybir.dt.from_np(a.dtype), kind="ExternalInput").ap() for name, a in arrays.items()]
    out = nc.dram_tensor("outT", (KT, P, T), _mybir.dt.float32, kind="ExternalOutput").ap()
    build(nc, *args, out)
    r = _run(nc, [arrays], core_ids=[0])
    return r.results[0]["outT"].reshape(D, T).T.reshape(1, T, D)
```
